# Optimizing a Trainium2 kernel written in Bass

```python
import jax, jax.numpy as jnp
from jax import lax
import numpy as np

D_MODEL = 1024
BATCH = 1
SEQ = 256
DEPTH = 1

HEAD_DIM = 64
N_Q_HEADS = 8
N_KV_HEADS = 2
Q_GROUP = N_Q_HEADS // N_KV_HEADS
Q_WIDTH = N_Q_HEADS * HEAD_DIM
KV_WIDTH = N_KV_HEADS * HEAD_DIM
AXIS_DIM = HEAD_DIM // 2
ROPE_THETA = 10000.0
Q_BLOCK = 128
GRID_W = 64
LRU_WIDTH = D_MODEL
LRU_BLOCKS = 16
LRU_BLOCK_W = LRU_WIDTH // LRU_BLOCKS
CONV_WIDTH = 4
CONV_PAD = (1, 2)
RG_C = 8.0
N_BRANCHES = 2
IN_WIDTH = Q_WIDTH + 2 * KV_WIDTH + 2 * LRU_WIDTH + N_BRANCHES * D_MODEL
SPLITS = (Q_WIDTH, Q_WIDTH + KV_WIDTH, Q_WIDTH + 2 * KV_WIDTH,
          Q_WIDTH + 2 * KV_WIDTH + LRU_WIDTH, Q_WIDTH + 2 * KV_WIDTH + 2 * LRU_WIDTH)
N_EXPERTS = 32
TOP_K = 4
D_FF = D_MODEL
SWIGLU_LIMIT = 7.0
SWIGLU_ALPHA = 1.702
DISPATCH_BLOCK = 256
NORM_EPS = 1e-6

kernel_name = 'hybrid_gqa_rglru_moe_encoder'

def rmsnorm(x, g):
    xf = x.astype(jnp.float32)
    y = xf * lax.rsqrt(jnp.mean(xf * xf, axis=-1, keepdims=True) + NORM_EPS)
    return (y * g.astype(jnp.float32)).astype(x.dtype)

def axial_rope_tables(S, dtype):
    rows = S // GRID_W
    row = jnp.repeat(jnp.arange(rows, dtype=jnp.int32), GRID_W).astype(jnp.float32)
    col = jnp.tile(jnp.arange(GRID_W, dtype=jnp.int32), rows).astype(jnp.float32)
    inv = ROPE_THETA ** (-jnp.arange(0, AXIS_DIM, 2, dtype=jnp.float32) / AXIS_DIM)
    ang_r = row[:, None] * inv[None, :]
    ang_c = col[:, None] * inv[None, :]
    f = lambda a: a[None, :, None, :].astype(dtype)
    return f(jnp.cos(ang_r)), f(jnp.sin(ang_r)), f(jnp.cos(ang_c)), f(jnp.sin(ang_c))

def rotate(x, cos, sin):
    x1, x2 = jnp.split(x, 2, axis=-1)
    return jnp.concatenate([x1 * cos - x2 * sin, x2 * cos + x1 * sin], axis=-1)

def apply_axial_rope(x, tables):
    cos_r, sin_r, cos_c, sin_c = tables
    return jnp.concatenate([rotate(x[..., :AXIS_DIM], cos_r, sin_r),
                            rotate(x[..., AXIS_DIM:], cos_c, sin_c)], axis=-1)

def block_attention(q, k, v):
    B, S = q.shape[0], q.shape[1]
    scale = HEAD_DIM ** -0.5
    qb = q.reshape(B, S // Q_BLOCK, Q_BLOCK, N_KV_HEADS, Q_GROUP, HEAD_DIM)
    qb = jnp.moveaxis(qb, 1, 0)

    def one_block(qblk):
        s = jnp.einsum('bqkgd,bskd->bkgqs', qblk, k).astype(jnp.float32) * scale
        p = jax.nn.softmax(s, axis=-1).astype(v.dtype)
        return jnp.einsum('bkgqs,bskd->bqkgd', p, v)

    o = lax.map(one_block, qb)
    return jnp.moveaxis(o, 0, 1).reshape(B, S, Q_WIDTH)

def depthwise_conv(x, w, b):
    C = x.shape[-1]
    y = lax.conv_general_dilated(x, w[:, None, :].astype(x.dtype), window_strides=(1,),
                                 padding=(CONV_PAD,), dimension_numbers=('NWC', 'WIO', 'NWC'),
                                 feature_group_count=C)
    return y + b

def block_diag(x, w, b):
    B, S, _ = x.shape
    xb = x.reshape(B, S, LRU_BLOCKS, LRU_BLOCK_W)
    y = jnp.einsum('bsnc,ncd->bsnd', xb, w) + b
    return y.reshape(B, S, LRU_WIDTH)

def linear_combine(earlier, later):
    a1, b1 = earlier
    a2, b2 = later
    return a1 * a2, a2 * b1 + b2

def rglru(x, wa, ba, wi, bi, lam, reverse):
    r = jax.nn.sigmoid(block_diag(x, wa, ba)).astype(jnp.float32)
    i = jax.nn.sigmoid(block_diag(x, wi, bi))
    log_a = RG_C * r * jax.nn.log_sigmoid(lam.astype(jnp.float32))
    a = jnp.exp(log_a)
    u = jnp.sqrt(-jnp.expm1(2.0 * log_a)) * (i * x).astype(jnp.float32)
    _, h = lax.associative_scan(linear_combine, (a, u), reverse=reverse, axis=1)
    return h.astype(x.dtype)

def token_mixer(h, w_in, b_in, q_norm_g, k_norm_g, conv_w, conv_b, lru_wa, lru_ba,
                lru_wi, lru_bi, lru_lambda, w_attn_o, w_lru_o, w_out):
    B, S, _ = h.shape
    proj = h @ w_in + b_in
    q, k, v, xr, yr, gate_logits = jnp.split(proj, SPLITS, axis=-1)
    tables = axial_rope_tables(S, h.dtype)
    q = apply_axial_rope(rmsnorm(q.reshape(B, S, N_Q_HEADS, HEAD_DIM), q_norm_g), tables)
    k = apply_axial_rope(rmsnorm(k.reshape(B, S, N_KV_HEADS, HEAD_DIM), k_norm_g), tables)
    v = v.reshape(B, S, N_KV_HEADS, HEAD_DIM)
    attn = block_attention(q, k, v)
    xc = depthwise_conv(xr, conv_w, conv_b)
    lru = (rglru(xc, lru_wa[0], lru_ba[0], lru_wi[0], lru_bi[0], lru_lambda[0], False)
           + rglru(xc, lru_wa[1], lru_ba[1], lru_wi[1], lru_bi[1], lru_lambda[1], True))
    rec = lru * jax.nn.gelu(yr, approximate=True)
    g_attn, g_rec = jnp.split(jax.nn.sigmoid(gate_logits), N_BRANCHES, axis=-1)
    merged = g_attn * (attn @ w_attn_o) + g_rec * (rec @ w_lru_o)
    return merged @ w_out

def moe_ffn(h, w_router, b_router, w_gu, b_gu, w_down, b_down):
    B, S, D = h.shape
    t = h.reshape(B * S, D)
    T = B * S
    A = T * TOP_K
    logits = (t @ w_router + b_router).astype(jnp.float32)
    top_val, top_idx = lax.top_k(logits, TOP_K)
    gates = jax.nn.softmax(top_val, axis=-1).astype(t.dtype)
    e_flat = top_idx.reshape(A).astype(jnp.int32)
    tok_flat = jnp.arange(A, dtype=jnp.int32) // TOP_K
    e_sorted, order = lax.sort((e_flat, jnp.arange(A, dtype=jnp.int32)), num_keys=2)
    tok_sorted = tok_flat[order]
    gate_sorted = gates.reshape(A)[order]
    counts = jnp.bincount(e_flat, length=N_EXPERTS)
    padded = (counts + DISPATCH_BLOCK - 1) // DISPATCH_BLOCK * DISPATCH_BLOCK
    start = jnp.cumsum(counts) - counts
    pend = jnp.cumsum(padded)
    pstart = pend - padded
    dest = pstart[e_sorted] + jnp.arange(A, dtype=jnp.int32) - start[e_sorted]
    n_blocks = (A + N_EXPERTS * (DISPATCH_BLOCK - 1) + DISPATCH_BLOCK - 1) // DISPATCH_BLOCK
    P = n_blocks * DISPATCH_BLOCK
    buf = jnp.zeros((P, D), t.dtype).at[dest].set(t[tok_sorted])
    blk_start = jnp.arange(n_blocks, dtype=jnp.int32) * DISPATCH_BLOCK
    blk_exp = jnp.minimum(jnp.searchsorted(pend, blk_start, side='right'), N_EXPERTS - 1)

    def expert_block(args):
        xb, e = args
        gu = xb @ w_gu[e] + b_gu[e]
        g, u = jnp.split(gu, 2, axis=-1)
        g = jnp.minimum(g, SWIGLU_LIMIT)
        u = jnp.clip(u, -SWIGLU_LIMIT, SWIGLU_LIMIT)
        act = g * jax.nn.sigmoid(SWIGLU_ALPHA * g) * (u + 1.0)
        return act @ w_down[e] + b_down[e]

    out_buf = lax.map(expert_block, (buf.reshape(n_blocks, DISPATCH_BLOCK, D), blk_exp))
    y_sorted = out_buf.reshape(P, D)[dest] * gate_sorted[:, None]
    y = jax.ops.segment_sum(y_sorted, tok_sorted, num_segments=T)
    return y.reshape(B, S, D)

def setup_inputs(seed: int = 0) -> dict:
    key = jax.random.key(seed)
    ks = jax.random.split(key, 24)
    f32 = jnp.float32
    nrm = lambda k, shape, fan_in: jax.random.normal(k, shape, f32) * (fan_in ** -0.5)
    small = lambda k, shape: 0.01 * jax.random.normal(k, shape, f32)
    gain = lambda k, shape: 1.0 + 0.05 * jax.random.normal(k, shape, f32)
    u = jax.random.uniform(ks[13], (DEPTH, 2, LRU_WIDTH), f32, 0.9, 0.999)
    s = u ** (1.0 / RG_C)
    lru_lambda = jnp.log(s) - jnp.log1p(-s)
    return {
        'x': jax.random.normal(ks[0], (BATCH, SEQ, D_MODEL), f32),
        'norm1_g': gain(ks[1], (DEPTH, D_MODEL)),
        'w_in': nrm(ks[2], (DEPTH, D_MODEL, IN_WIDTH), D_MODEL),
        'b_in': small(ks[3], (DEPTH, IN_WIDTH)),
        'q_norm_g': gain(ks[4], (DEPTH, HEAD_DIM)),
        'k_norm_g': gain(ks[5], (DEPTH, HEAD_DIM)),
        'conv_w': nrm(ks[6], (DEPTH, CONV_WIDTH, LRU_WIDTH), CONV_WIDTH),
        'conv_b': small(ks[7], (DEPTH, LRU_WIDTH)),
        'lru_wa': nrm(ks[8], (DEPTH, 2, LRU_BLOCKS, LRU_BLOCK_W, LRU_BLOCK_W), LRU_BLOCK_W),
        'lru_ba': small(ks[9], (DEPTH, 2, LRU_BLOCKS, LRU_BLOCK_W)),
        'lru_wi': nrm(ks[10], (DEPTH, 2, LRU_BLOCKS, LRU_BLOCK_W, LRU_BLOCK_W), LRU_BLOCK_W),
        'lru_bi': small(ks[11], (DEPTH, 2, LRU_BLOCKS, LRU_BLOCK_W)),
        'lru_lambda': lru_lambda,
        'w_attn_o': nrm(ks[14], (DEPTH, Q_WIDTH, D_MODEL), Q_WIDTH),
        'w_lru_o': nrm(ks[15], (DEPTH, LRU_WIDTH, D_MODEL), LRU_WIDTH),
        'w_out': nrm(ks[16], (DEPTH, D_MODEL, D_MODEL), D_MODEL),
        'norm2_g': gain(ks[17], (DEPTH, D_MODEL)),
        'w_router': nrm(ks[18], (DEPTH, D_MODEL, N_EXPERTS), D_MODEL),
        'b_router': small(ks[19], (DEPTH, N_EXPERTS)),
        'w_gu': nrm(ks[20], (DEPTH, N_EXPERTS, D_MODEL, 2 * D_FF), D_MODEL),
        'b_gu': small(ks[21], (DEPTH, N_EXPERTS, 2 * D_FF)),
        'w_down': nrm(ks[22], (DEPTH, N_EXPERTS, D_FF, D_MODEL), D_FF),
        'b_down': small(ks[23], (DEPTH, N_EXPERTS, D_MODEL)),
        'final_g': gain(ks[12], (D_MODEL,)),
    }

def reference(x, norm1_g, w_in, b_in, q_norm_g, k_norm_g, conv_w, conv_b, lru_wa, lru_ba,
              lru_wi, lru_bi, lru_lambda, w_attn_o, w_lru_o, w_out, norm2_g, w_router,
              b_router, w_gu, b_gu, w_down, b_down, final_g):
    for l in range(DEPTH):
        h = rmsnorm(x, norm1_g[l])
        x = x + token_mixer(h, w_in[l], b_in[l], q_norm_g[l], k_norm_g[l], conv_w[l], conv_b[l],
                            lru_wa[l], lru_ba[l], lru_wi[l], lru_bi[l], lru_lambda[l],
                            w_attn_o[l], w_lru_o[l], w_out[l])
        h = rmsnorm(x, norm2_g[l])
        x = x + moe_ffn(h, w_router[l], b_router[l], w_gu[l], b_gu[l], w_down[l], b_down[l])
    return rmsnorm(x, final_g)


_drawn_inputs = setup_inputs


def setup_inputs(seed=0):
    import zlib

    import numpy as np

    out = dict(_drawn_inputs(seed))
    spreads = {}
    factors = {'q_norm_g': 3.595,
     'k_norm_g': 3.316,
     'lru_ba': 22.193,
     'lru_bi': 13.862,
     'b_gu': 8.0,
     'b_down': 8.0}
    for name, (base, spread) in spreads.items():
        noise = np.random.default_rng([zlib.crc32(name.encode()), seed]).standard_normal(out[name].shape)
        drawn = base * np.exp(spread * noise) if base else spread * noise
        out[name] = __import__('jax').numpy.asarray(drawn.astype(out[name].dtype))
    for name, factor in factors.items():
        out[name] = (out[name] * factor).astype(out[name].dtype)
    return out
```

```python
import numpy as np
import concourse.bass as bass
from concourse import mybir
from contextlib import ExitStack

P = 128
D = 1024
TOK = 256
T = TOK // P
KD = D // P
HD = 64
NQ, NKV = 8, 2
NH = NQ + NKV
QW, KVW = NQ * HD, NKV * HD
QKV = QW + 2 * KVW
GRID_W = 64
THETA = 10000.0
EPS = 1e-6
RG_C = 8.0
TAPS, PAD_L, PAD_R = 4, 1, 2
NE, TOPK = 32, 4
FF = 1024
LIMIT, ALPHA = 7.0, 1.702
BANK = 512
CH = 4096
SLOTS = 6
PRE = 15
CAP = 64
ROUNDS = TOK // CAP
FAR = 4096.0

C_G1, C_G2, C_BIN, C_CW, C_CB, C_LB, C_LAM, C_COS, C_SIN, C_BGU, C_WR = (
    0, 8, 16, 48, 80, 88, 120, 136, 264, 392, 904)
C_ALL = C_WR + KD * NE


def encoder_layer(nc, x, consts, squares, rows, pre, w_gu, w_down, b_down, out):
    f32, i32, u32 = mybir.dt.float32, mybir.dt.int32, mybir.dt.uint32
    ALU, ACT, AX = mybir.AluOpType, mybir.ActivationFunctionType, mybir.AxisListType

    ctx = ExitStack()
    with ctx:
        def sb(name, shape, dt=f32):
            return ctx.enter_context(nc.sbuf_tensor(name, shape, dt))

        def sem(name):
            return ctx.enter_context(nc.semaphore(name))

        ring = sb("ring", [P, SLOTS, CH])
        x_sb = sb("x_sb", [P, T, D])
        hn = sb("hn", [P, T, D])
        hT = sb("hT", [P, KD, TOK])
        xr = sb("xr", [P, KD, PAD_L + TOK + PAD_R])
        xc = sb("xc", [P, KD, TOK])
        gelu = sb("gelu", [P, KD, TOK])
        gR = sb("gR", [P, KD, TOK])
        lru = sb("lru", [P, 4, 2048])
        qkv = sb("qkv", [P, T, QKV])
        qT = sb("qT", [P, NQ // 2, TOK])
        kT = sb("kT", [P, NKV, TOK])
        prob = sb("prob", [P, 2, T, TOK])
        probT = sb("probT", [P, 2, T, TOK])
        attnT = sb("attnT", [P, QW // P, TOK])
        cst = sb("cst", [P, C_ALL])
        sq = sb("sq", [P, 4, P])
        bqkv = sb("bqkv", [P, QKV])
        gains = sb("gains", [P, NH * HD])
        brt = sb("brt", [P, NE])
        small = sb("small", [P, 256])
        gateT = sb("gateT", [NE, TOK])

        ident, upper, ones, slotno = (sq[:, i, :] for i in range(4))
        hb = cst[:, C_BIN + 16:C_BIN + 32]
        gA = hn[:, :, :].rearrange("p t d -> p (t d)").rearrange("p (k n) -> p k n", k=KD)

        col = [0]

        def scratch(n):
            col[0] += n
            return small[:, col[0] - n:col[0]]

        ssum, rstd = scratch(2), scratch(2)
        qk_rstd = scratch(T * NH)
        lam_c = scratch(16)
        lam_t = [scratch(16) for _ in range(4)]
        neg_max, exp_sum = scratch(4), scratch(4)

        lruR, lruI, lruD, lruS = (lru[:, i, :] for i in range(4))
        mergedT = lruR.rearrange("p (k n) -> p k n", k=KD)
        m_a, m_r = lruD[:, 0:512], lruD[:, 512:1024]
        h2T = lruI.rearrange("p (k n) -> p k n", k=KD)
        gu_sb = lruS[:, 0:1024]
        gub = lruS[:, 1024:2048]
        xgT = lruD[:, 0:512].rearrange("p (k n) -> p k n", k=KD)
        g_cl, sig, act1 = lruD[:, 512:1024], lruD[:, 1024:1536], lruD[:, 1536:2048]
        u_cl = lruR[:, 0:512]
        actT = lruR[:, 512:1024].rearrange("p (k n) -> p k n", k=KD)
        out_sb = lruR[:, 1024:1536]
        sel_next = lruR[:, 1536:1536 + T * CAP].rearrange("p (t n) -> p t n", t=T)
        sel_gate = lruR[:, 1664:1664 + T * P].rearrange("p (t n) -> p t n", t=T)
        sgT = xc[:, 0, :].rearrange("p (t n) -> p t n", t=T)
        NCOL = (ROUNDS + 1) * NE
        pflat = prob[:, :, :, :].rearrange("p a t n -> p (a t n)")
        rank_col = pflat[:, 0:T * NCOL].rearrange("p (t n) -> p t n", t=T)
        gate_col = pflat[:, T * NCOL:2 * T * NCOL].rearrange("p (t n) -> p t n", t=T)
        tflat = probT[:, :, :, :].rearrange("p a t n -> p (a t n)")
        logit = tflat[:, 0:64].rearrange("p (t e) -> p t e", t=T)
        top8 = tflat[:, 64:80].rearrange("p (t k) -> p t k", t=T)
        idx_f = tflat[:, 80:96].rearrange("p (t k) -> p t k", t=T)
        ex4 = tflat[:, 96:104].rearrange("p (t k) -> p t k", t=T)
        g4 = tflat[:, 104:112].rearrange("p (t k) -> p t k", t=T)
        nmax, esum, einv = tflat[:, 112:114], tflat[:, 114:116], tflat[:, 116:118]
        hot = tflat[:, 128:384].rearrange("p (t k e) -> p t k e", t=T, k=TOPK)
        hotg = tflat[:, 384:640].rearrange("p (t k e) -> p t k e", t=T, k=TOPK)
        mask = tflat[:, 640:704].rearrange("p (t e) -> p t e", t=T)
        gate = tflat[:, 704:768].rearrange("p (t e) -> p t e", t=T)
        ranked = tflat[:, 768:832].rearrange("p (t e) -> p t e", t=T)
        cmax, rnd, rnd2 = tflat[0:1, 832:833], tflat[0:1, 833:834], tflat[0:1, 834:835]
        idx_u = sb("idx_u", [P, T, 8], u32)
        passes = sb("passes", [1, 1], i32)
        fin_g = gelu[:, 0:4, :].rearrange("p k n -> p (k n)")
        bdn = gelu[0:NE, 4:8, :].rearrange("p k n -> p (k n)")

        ps = ctx.enter_context(nc.psum_tensor("ps", [P, 8, BANK], f32))

        def half(bank, h):
            return ps[:, bank, h * TOK:(h + 1) * TOK]

        x_in, cst_in, sq_in, bias_in, late_in, out_done_dma = (
            sem(n) for n in ("x_in", "cst_in", "sq_in", "bias_in", "late_in", "out_stored"))
        slot_full = [sem(f"slot_full{i}") for i in range(SLOTS)]
        chunk_used = [sem(f"chunk_used{j}") for j in range(SLOTS)]
        v_step, a_step = sem("v_step"), sem("a_step")
        sq_sum, var_inv, rstd_ok, normed = sem("sq_sum"), sem("var_inv"), sem("rstd_ok"), sem("normed")
        tposed, hT_v, hT_a = sem("tposed"), sem("hT_v"), sem("hT_a")
        group_done, group_read = sem("group_done"), sem("group_read")
        qkv_done, qkv_ok = sem("qkv_done"), sem("qkv_ok")
        conv_ok, conv_half = sem("conv_ok"), sem("conv_half")
        margins = sem("margins")
        gate_ps, gate_read, lru_t, lru_s, lru_unit = (
            sem("lru_gate_ps"), sem("lru_gate_read"), sem("lru_t"), sem("lru_s"), sem("lru_unit"))
        lam_e, lam_ok, hb_ok = sem("lam_exp"), sem("lam_ok"), sem("half_bias_ok")
        qk_inv, qk_rs, rot_ok, qk_tp, qk_cp = sem("qk_inv"), sem("qk_rs"), sem("rot_ok"), sem("qk_tposed"), sem("qk_copied")
        score_ps, max_ok, exp_ok, prob_ok, pT_ps, pT_ok, pv_ps, attn_ok = (
            sem(n) for n in ("score_ps", "max_ok", "exp_ok", "prob_ok", "probT_ps", "probT_ok", "pv_ps", "attn_ok"))
        branch_ps, merged_ok, mixed_ps, x2_ok = sem("branch_ps"), sem("merged_ok"), sem("mixed"), sem("x2_ok")
        logit_ps, top_ok, ex_ok, mask_ok, rank_ps, gateT_ps, gateT_ok, cols_ok, passes_ok, ybias = (
            sem(n) for n in ("logit_ps", "top_ok", "top_exp_ok", "mask_ok", "rank_ps", "gateT_ps", "gateT_ok",
                             "cols_ok", "passes_ok", "y_bias"))
        sel_ok, xg_ps, xg_ok, gu_v, gu_a, tp_ps, tp_read, sgate_ok, sg_ps, sg_ok = (
            sem(n) for n in ("sel_ok", "xg_ps", "xg_ok", "gu_copied_v", "gu_copied_a", "tp_ps", "tp_read",
                             "sel_gate_ok", "sgT_ps", "sgT_ok"))
        g_ok, sig_ok, u_ok, a1_ok, act_ok, out_ok, y_ok = (
            sem(n) for n in ("g_clamped", "sigmoid_ok", "u_clamped", "gated_ok", "act_ok", "out_ok", "y_ok"))
        x3_ok, fin_ok = sem("x3_ok"), sem("fin_ok")

        block = ctx.enter_context(nc.Block())

        gu_chunk = w_gu.rearrange("e (p j r) n -> e j p (r n)", j=4, r=2)
        dn_chunk = w_down.rearrange("e (p j r) n -> e j p (r n)", j=2, r=4)

        def slot_of(chunk):
            return chunk % SLOTS

        def use_of(chunk):
            return chunk // SLOTS

        CONSUMED = ([(group_done, 4), (group_done, 8), (qkv_done, T), (gate_ps, 32)]
                    + [(group_done, 12 + 4 * i) for i in range(6)]
                    + [(branch_ps, KD)] * 3 + [(mixed_ps, 1), (mixed_ps, 2)])
        EXP = [(slot_of(PRE + j), use_of(PRE + j)) for j in range(SLOTS)]

        @block.sync
        def _(sp):
            for t in range(T):
                sp.dma_start(x_sb[:, t, :], x[t * P:(t + 1) * P, :]).then_inc(x_in, 16)
            for c in range(PRE):
                if c >= SLOTS:
                    sp.wait_ge(*CONSUMED[c - SLOTS])
                sp.dma_start(ring[:, slot_of(c), :], pre[c, :, :]).then_inc(slot_full[slot_of(c)], 16)
            for j, (s, u) in enumerate(EXP):
                sp.wait_ge(*CONSUMED[PRE + j - SLOTS])
                src = gu_chunk[0, j] if j < 4 else dn_chunk[0, j - 4]
                sp.dma_start(ring[:, s, :], src).then_inc(slot_full[s], 16)
            sp.wait_ge(passes_ok, 1)
            n_pass = sp.value_load(passes[0:1, 0:1], min_val=NE, max_val=NE * ROUNDS)
            with sp.Fori(1, n_pass) as n:
                e = sp.snap(sp.to_reg(n & (NE - 1)), min_val=0, max_val=NE - 1)
                for j, (s, u) in enumerate(EXP):
                    src = gu_chunk[bass.ds(e, 1), j] if j < 4 else dn_chunk[bass.ds(e, 1), j - 4]
                    sp.wait_ge(chunk_used[j], n)
                    sp.dma_start(ring[:, s, :], src.rearrange("o p n -> (o p) n")).then_inc(slot_full[s], 16)
            for t in range(T):
                sp.wait_ge(fin_ok, t + 1)
                sp.dma_start(out[t * P:(t + 1) * P, :], x_sb[:, t, :]).then_inc(out_done_dma, 16)
            sp.wait_ge(out_done_dma, 16 * T)

        @block.scalar
        def _(act):
            act.dma_start(sq[:, :, :], squares).then_inc(sq_in, 16)
            act.dma_start(cst[:, :], consts).then_inc(cst_in, 16)
            act.dma_start(bqkv[:, :], rows[0:1, 0:QKV].to_broadcast([P, QKV])).then_inc(bias_in, 16)
            for h in range(NH):
                o = QKV + (0 if h < NQ else HD)
                act.dma_start(gains[:, h * HD:(h + 1) * HD], rows[0:1, o:o + HD].to_broadcast([P, HD])).then_inc(bias_in, 16)
            o = QKV + 2 * HD
            act.dma_start(brt[:, :], rows[0:1, o:o + NE].to_broadcast([P, NE])).then_inc(late_in, 16)

            def norm_rows(turn, ready, value):
                for t in range(T):
                    act.wait_ge(ready, value(t))
                    dst = hn[:, t, :] if turn == 0 else lru[:, 2, 0:D] if t == 0 else lru[:, 3, 0:D]
                    nc.scalar.activation(dst, x_sb[:, t, :], ACT.Square,
                                         accum_out=ssum[:, t:t + 1]).then_inc(sq_sum, 1)
                act.wait_ge(var_inv, turn + 1)
                nc.scalar.activation(rstd, ssum, ACT.Sqrt).then_inc(rstd_ok, 1)

            def scaled_copy(turn, g, dst, tp0):
                for k in range(4, 8):
                    act.wait_ge(tposed, 8 * turn + k // 2 * 2 + 2)
                    nc.scalar.activation(dst[:, k, :], half(tp0 + k // 2, k % 2), ACT.Copy,
                                         scale=cst[:, g + k:g + k + 1]).then_inc(hT_a, 1)

            def group(i):
                act.wait_ge(group_done, i // 2 * 2 + 2)
                src = half(4 + (i // 2) % 2, i % 2)
                if i < 8:
                    if i == 0:
                        act.wait_ge(margins, 1)
                    nc.scalar.activation(xr[:, i, PAD_L:PAD_L + TOK], src, ACT.Identity,
                                         bias=cst[:, C_BIN + i:C_BIN + i + 1]).then_inc(group_read, 1)
                elif i < 16:
                    nc.scalar.activation(gelu[:, i - 8, :], src, ACT.Gelu_apprx_tanh,
                                         bias=cst[:, C_BIN + i:C_BIN + i + 1]).then_inc(group_read, 1)
                else:
                    dst = gA[:, i - 16, :] if i < 24 else gR[:, i - 24, :]
                    nc.scalar.activation(dst, src, ACT.Tanh, scale=0.5,
                                         bias=hb[:, i - 16:i - 15]).then_inc(group_read, 1)

            def lru_gates(u):
                if u == 1:
                    act.wait_ge(lru_unit, 1)
                for c in range(4):
                    for m in range(4):
                        n = 16 * u + 4 * c + m
                        act.wait_ge(gate_ps, n // 2 * 2 + 2)
                        dst = (lruR if m % 2 == 0 else lruI)[:, (m // 2 * 4 + c) * TOK:(m // 2 * 4 + c + 1) * TOK]
                        b = C_LB + m * 8 + 4 * u + c
                        nc.scalar.activation(dst, half(6 + (n % 4) // 2, n % 2), ACT.Sigmoid,
                                             bias=cst[:, b:b + 1]).then_inc(gate_read, 1)
                act.wait_ge(gate_read, 16 * (u + 1))
                act.wait_ge(lam_ok, 1)
                for d in range(2):
                    for c in range(4):
                        o = (4 * d + c) * TOK
                        k = 8 * d + 4 * u + c
                        nc.scalar.activation(lruR[:, o:o + TOK], lruR[:, o:o + TOK], ACT.Tanh,
                                             scale=lam_c[:, k:k + 1]).then_inc(lru_t, 1)
                act.wait_ge(lru_t, 8 * (u + 1))
                if u == 0:
                    act.wait_ge(rot_ok, T)
                nc.scalar.activation(lruS, lruR, ACT.Sqrt, scale=-4.0).then_inc(lru_s, 1)

            norm_rows(0, x_in, lambda t: 16 * T)
            act.wait_ge(cst_in, 16)
            scaled_copy(0, C_G1, hT, 0)
            act.wait_ge(lam_e, 1)
            nc.scalar.activation(lam_t[1], lam_t[0], ACT.Exp, scale=-1.0).then_inc(lam_e, 1)
            for i in range(8):
                group(i)
            act.wait_ge(qk_inv, 1)
            nc.scalar.activation(qk_rstd, qk_rstd, ACT.Sqrt).then_inc(qk_rs, 1)
            lru_gates(0)
            for i in range(8, 12):
                group(i)
            for j in range(2):
                act.wait_ge(qk_tp, j + 1)
                nc.scalar.activation(qT[:, 2 * j:2 * j + 2, :].rearrange("p a n -> p (a n)"), ps[:, j, :],
                                     ACT.Copy).then_inc(qk_cp, 1)
            act.wait_ge(qk_tp, 3)
            nc.scalar.activation(kT[:, :, :].rearrange("p a n -> p (a n)"), ps[:, 2, :], ACT.Copy).then_inc(qk_cp, 1)
            for i in range(12, 16):
                group(i)
            lru_gates(1)
            act.wait_ge(hb_ok, 1)
            for i in range(16, 32):
                group(i)
                s = i - 20
                if 0 <= s - 2 < NQ:
                    h = s - 2
                    act.wait_ge(pT_ps, h + 1)
                    nc.scalar.activation(probT[:, h % 2, :, :].rearrange("p a n -> p (a n)"), ps[:, 2, :],
                                         ACT.Copy).then_inc(pT_ok, 1)
                if 0 <= s < NQ:
                    act.wait_ge(max_ok, s + 1)
                    for t in range(T):
                        b = (s % 2) * T + t
                        nc.scalar.activation(prob[:, s % 2, t, :], ps[:, s % 2, t * TOK:(t + 1) * TOK], ACT.Exp,
                                             bias=neg_max[:, b:b + 1], scale=HD ** -0.5,
                                             accum_out=exp_sum[:, b:b + 1]).then_inc(exp_ok, 1)
            act.wait_ge(lru_unit, 2)
            act.dma_start(fin_g, rows[0:1, o + NE:o + NE + D].to_broadcast([P, D])).then_inc(late_in, 16)
            act.dma_start(bdn, b_down).then_inc(late_in, 16)
            norm_rows(1, x2_ok, lambda t: 2 * t + 2)
            scaled_copy(1, C_G2, h2T, 4)
            for t in range(T):
                act.wait_ge(top_ok, 1)
                nc.scalar.activation(ex4[:, t, :], top8[:, t, 0:TOPK], ACT.Exp, bias=nmax[:, t:t + 1],
                                     accum_out=esum[:, t:t + 1]).then_inc(ex_ok, 1)

            act.wait_ge(passes_ok, 1)
            n_pass = act.value_load(passes[0:1, 0:1], min_val=NE, max_val=NE * ROUNDS)
            with act.Fori(0, n_pass) as n:
                n1 = act.snap(n + 1)
                act.wait_ge(chunk_used[3], n1)
                nc.scalar.activation(gu_sb[:, BANK:2 * BANK], ps[:, 5, :], ACT.Copy).then_inc(gu_a, 1)
                act.wait_ge(g_ok, n1)
                nc.scalar.activation(sig, g_cl, ACT.Sigmoid, scale=ALPHA).then_inc(sig_ok, 1)
                act.wait_ge(chunk_used[5], n1)
                nc.scalar.activation(out_sb, ps[:, 6, :], ACT.Copy).then_inc(out_ok, 1)

            norm_rows(2, x3_ok, lambda t: 2 * t + 2)

        @block.vector
        def _(dve):
            steps = [0]

            def link(ins):
                steps[0] += 1
                ins.then_inc(v_step, 1)
                dve.wait_ge(v_step, steps[0])

            def inverse_variance(turn, total, n, value):
                dve.wait_ge(total, value)
                link(nc.vector.tensor_scalar(ssum, ssum, 1.0 / n, EPS, ALU.mult, ALU.add))
                nc.vector.reciprocal(ssum, ssum).then_inc(var_inv, 1)

            def norm_apply(turn):
                dve.wait_ge(rstd_ok, turn + 1)
                for t in range(T):
                    nc.vector.tensor_scalar(hn[:, t, :], x_sb[:, t, :], rstd[:, t:t + 1], None,
                                            ALU.mult).then_inc(normed, 1)

            def scaled_copy(turn, g, dst, tp0):
                for b in range(2):
                    dve.wait_ge(tposed, 8 * turn + 2 * b + 2)
                    nc.vector.tensor_tensor(
                        dst[:, 2 * b:2 * b + 2, :], ps[:, tp0 + b, :].rearrange("p (k n) -> p k n", k=2),
                        cst[:, g + 2 * b:g + 2 * b + 2].unsqueeze(2).to_broadcast([P, 2, TOK]),
                        ALU.mult).then_inc(hT_v, 1)

            nc.vector.memset(xr[:, :, 0:PAD_L], 0.0)
            nc.vector.memset(xr[:, :, PAD_L + TOK:], 0.0).then_inc(margins, 1)
            inverse_variance(0, sq_sum, D, T)
            norm_apply(0)
            dve.wait_ge(cst_in, 16)
            scaled_copy(0, C_G1, hT, 0)

            lam = cst[:, C_LAM:C_LAM + 16]
            link(nc.vector.tensor_scalar(lam_t[0], lam, -1.0, None, ALU.mult))
            nc.vector.tensor_tensor(lam_t[0], lam_t[0], lam, ALU.max).then_inc(lam_e, 1)
            link(nc.vector.tensor_scalar(hb, hb, 0.5, None, ALU.mult))
            dve.wait_ge(lam_e, 2)
            link(nc.vector.tensor_scalar(lam_t[2], lam_t[1], 2.0, None, ALU.add))
            link(nc.vector.reciprocal(lam_t[2], lam_t[2]))
            link(nc.vector.tensor_tensor(lam_t[1], lam_t[1], lam_t[2], ALU.mult))
            link(nc.vector.tensor_tensor(lam_t[2], lam_t[1], lam_t[1], ALU.mult))
            link(nc.vector.tensor_scalar(lam_t[3], lam_t[2], 1.0 / 17, 1.0 / 15, ALU.mult, ALU.add))
            for q in (13, 11, 9, 7, 5, 3, 1):
                link(nc.vector.tensor_tensor(lam_t[3], lam_t[3], lam_t[2], ALU.mult))
                link(nc.vector.tensor_scalar(lam_t[3], lam_t[3], 1.0 / q, None, ALU.add))
            link(nc.vector.tensor_tensor(lam_t[3], lam_t[3], lam_t[1], ALU.mult))
            link(nc.vector.tensor_scalar(lam_t[0], lam, 0.0, RG_C / 2, ALU.min, ALU.mult))
            link(nc.vector.tensor_scalar(lam_t[3], lam_t[3], 2 * RG_C / 2, None, ALU.mult))
            nc.vector.tensor_tensor(lam_c, lam_t[0], lam_t[3], ALU.subtract).then_inc(lam_ok, 1)
            nc.vector.tensor_scalar(hb, hb, 1.0, None, ALU.mult).then_inc(hb_ok, 1)

            for c in range(KD):
                dve.wait_ge(group_read, c + 1)
                w = [cst[:, C_CW + 8 * j + c:C_CW + 8 * j + c + 1] for j in range(TAPS)]
                b = cst[:, C_CB + c:C_CB + c + 1]
                link(nc.vector.tensor_scalar(xc[:, c, :], xr[:, c, 0:TOK], w[0], b, ALU.mult, ALU.add))
                for j in range(1, TAPS):
                    ins = nc.vector.scalar_tensor_tensor(out=xc[:, c, :], in0=xr[:, c, j:j + TOK], scalar=w[j],
                                                         in1=xc[:, c, :], op0=ALU.mult, op1=ALU.add)
                    if j < TAPS - 1:
                        link(ins)
                    else:
                        ins.then_inc(conv_ok, 1)

            dve.wait_ge(bias_in, 16 * (1 + NH))
            for n in range(2 * T):
                part, t = n // T, n % T
                dve.wait_ge(qkv_done, n + 1)
                w = QW if part == 0 else 2 * KVW
                o = 0 if part == 0 else QW
                nc.vector.tensor_tensor(qkv[:, t, o:o + w], ps[:, 2 * t + part, 0:w], bqkv[:, o:o + w],
                                        ALU.add).then_inc(qkv_ok, 1)
            dve.wait_ge(qkv_ok, 2 * T)
            E2 = T * NH * HD
            qk4 = qkv[:, :, 0:NH * HD].rearrange("p t (h d) -> p t h d", h=NH)
            work = lru[:, 2:4, :].rearrange("p a n -> p (a n)")
            w1, w2, w3 = (work[:, i * E2:(i + 1) * E2] for i in range(3))
            v1, v2, v3 = (w.rearrange("p (t h d) -> p t h d", t=T, h=NH) for w in (w1, w2, w3))
            link(nc.vector.tensor_tensor(v1, qk4, qk4, ALU.mult))
            link(nc.vector.tensor_reduce(qk_rstd, w1.rearrange("p (g d) -> p g d", d=HD), AX.X, ALU.add))
            link(nc.vector.tensor_scalar(qk_rstd, qk_rstd, 1.0 / HD, EPS, ALU.mult, ALU.add))
            nc.vector.reciprocal(qk_rstd, qk_rstd).then_inc(qk_inv, 1)
            dve.wait_ge(qk_rs, 1)
            for t in range(T):
                r = qk_rstd[:, t * NH:(t + 1) * NH].unsqueeze(2).to_broadcast([P, NH, HD])
                link(nc.vector.tensor_tensor(v1[:, t], qk4[:, t], r, ALU.mult))
                link(nc.vector.tensor_tensor(v1[:, t], v1[:, t], gains[:, :].rearrange("p (h d) -> p h d", h=NH),
                                             ALU.mult))
                cos = cst[:, C_COS + t * HD:C_COS + (t + 1) * HD].unsqueeze(1).to_broadcast([P, NH, HD])
                link(nc.vector.tensor_tensor(v2[:, t], v1[:, t], cos, ALU.mult))
                Q4 = HD // 4
                s5 = v1[:, t].rearrange("p h (a b i) -> p h a b i", a=2, b=2)
                d5 = v3[:, t].rearrange("p h (a b i) -> p h a b i", a=2, b=2)
                for b in range(2):
                    for a in range(2):
                        o = C_SIN + t * HD + (2 * a + b) * Q4
                        sin = cst[:, o:o + Q4].unsqueeze(1).to_broadcast([P, NH, Q4])
                        nc.vector.tensor_tensor(d5[:, :, a, b, :], s5[:, :, a, 1 - b, :], sin,
                                                ALU.mult).then_inc(v_step, 1)
                        steps[0] += 1
                dve.wait_ge(v_step, steps[0])
                link(nc.vector.tensor_tensor(qk4[:, t], v2[:, t], v3[:, t], ALU.add))
            kd = w1[:, 0:T * NKV * P].rearrange("p (t g r d) -> p t g r d", t=T, g=NKV, r=2)
            for t in range(T):
                ins = nc.vector.tensor_copy(
                    kd[:, t], qkv[:, t, QW:QW + KVW].rearrange("p (g d) -> p g d", g=NKV).unsqueeze(2)
                    .to_broadcast([P, NKV, 2, HD]))
                ins.then_inc(rot_ok, 1)

            def lru_unit_work(u):
                rows = lambda b: b.rearrange("p (d c n) -> p d c n", d=2, c=4)
                x4 = xc[:, 4 * u:4 * u + 4, :]
                if u == 0:
                    dve.wait_ge(qk_tp, 3)
                dve.wait_ge(lru_t, 8 * (u + 1))
                link(nc.vector.tensor_scalar(lruD, lruR, -1.0, 1.0, ALU.mult, ALU.add))
                link(nc.vector.reciprocal(lruD, lruD))
                for d in range(2):
                    link(nc.vector.tensor_tensor(rows(lruI)[:, d], rows(lruI)[:, d], x4, ALU.mult))
                dve.wait_ge(lru_s, u + 1)
                link(nc.vector.scalar_tensor_tensor(out=lruR, in0=lruR, scalar=1.0, in1=lruD, op0=ALU.add,
                                                    op1=ALU.mult))
                link(nc.vector.tensor_tensor(lruS, lruS, lruD, ALU.mult))
                link(nc.vector.tensor_tensor(lruI, lruI, lruS, ALU.mult))
                for c in range(4):
                    for d in range(2):
                        a, b, h = rows(lruR)[:, d, c, :], rows(lruI)[:, d, c, :], rows(lruD)[:, d, c, :]
                        if d == 1:
                            a, b, h = a[:, ::-1], b[:, ::-1], h[:, ::-1]
                        nc.vector.tensor_tensor_scan(h, a, b, 0.0, ALU.mult, ALU.add).then_inc(v_step, 1)
                        steps[0] += 1
                dve.wait_ge(v_step, steps[0])
                link(nc.vector.tensor_tensor(x4, rows(lruD)[:, 0], rows(lruD)[:, 1], ALU.add))
                if u == 0:
                    dve.wait_ge(group_read, 12)
                else:
                    dve.wait_ge(group_read, 16)
                nc.vector.tensor_tensor(x4, x4, gelu[:, 4 * u:4 * u + 4, :], ALU.mult).then_inc(lru_unit, 1)

            lru_unit_work(0)
            lru_unit_work(1)

            def head_max(h):
                b = (h % 2) * T
                dve.wait_ge(score_ps, h + 1)
                link(nc.vector.tensor_reduce(neg_max[:, b:b + T], ps[:, h % 2, :].rearrange("p (t n) -> p t n", t=T),
                                             AX.X, ALU.max))
                nc.vector.tensor_scalar(neg_max[:, b:b + T], neg_max[:, b:b + T], -(HD ** -0.5), None,
                                        ALU.mult).then_inc(max_ok, 1)

            def head_norm(h):
                b = (h % 2) * T
                dve.wait_ge(exp_ok, T * (h + 1))
                link(nc.vector.reciprocal(exp_sum[:, b:b + T], exp_sum[:, b:b + T]))
                for t in range(T):
                    nc.vector.tensor_scalar(prob[:, h % 2, t, :], prob[:, h % 2, t, :], exp_sum[:, b + t:b + t + 1],
                                            None, ALU.mult).then_inc(prob_ok, 1)

            def pair_out(j):
                dve.wait_ge(pv_ps, 2 * j + 2)
                nc.vector.tensor_copy(attnT[:, j, :], half(3, 0)).then_inc(attn_ok, 1)

            for s in range(NQ + 3):
                if s < NQ:
                    head_max(s)
                    head_norm(s)
                if s >= 3 and (s - 3) % 2 == 1:
                    pair_out((s - 3) // 2)

            for g in range(KD):
                o = (g % 2) * TOK
                dve.wait_ge(branch_ps, g + 1)
                nc.vector.scalar_tensor_tensor(out=m_a[:, o:o + TOK], in0=gA[:, g, :], scalar=1.0,
                                               in1=half(4 + g % 2, 0), op0=ALU.add, op1=ALU.mult)
                link(nc.vector.scalar_tensor_tensor(out=m_r[:, o:o + TOK], in0=gR[:, g, :], scalar=1.0,
                                                    in1=half(4 + g % 2, 1), op0=ALU.add, op1=ALU.mult))
                nc.vector.tensor_tensor(mergedT[:, g, :], m_a[:, o:o + TOK], m_r[:, o:o + TOK],
                                        ALU.add).then_inc(merged_ok, 1)
            dve.wait_ge(mixed_ps, 2)
            for n in range(2 * T):
                t, o = n // 2, (n % 2) * BANK
                nc.vector.scalar_tensor_tensor(out=x_sb[:, t, o:o + BANK], in0=ps[:, n, :], scalar=0.5,
                                               in1=x_sb[:, t, o:o + BANK], op0=ALU.mult, op1=ALU.add).then_inc(x2_ok, 1)
            inverse_variance(1, sq_sum, D, 2 * T)
            norm_apply(1)
            scaled_copy(1, C_G2, h2T, 4)

            link(nc.vector.memset(rank_col[:, :, :], -1.0))
            dve.wait_ge(late_in, 48)
            dve.wait_ge(logit_ps, 1)
            link(nc.vector.tensor_tensor(logit, ps[:, 0, 0:T * NE].rearrange("p (t e) -> p t e", t=T),
                                         brt[:, :].unsqueeze(1).to_broadcast([P, T, NE]), ALU.add))
            for t in range(T):
                link(nc.vector.max(top8[:, t, :], logit[:, t, :]))
                link(nc.vector.max_index(idx_u[:, t, :], top8[:, t, :], logit[:, t, :]))
            nc.vector.tensor_scalar(nmax.unsqueeze(2), top8[:, :, 0:1], -1.0, None, ALU.mult).then_inc(top_ok, 1)
            link(nc.vector.tensor_copy(idx_f, idx_u[:, :, :]))
            expert_no = slotno[:, 0:NE].unsqueeze(1).to_broadcast([P, TOPK, NE])
            for t in range(T):
                link(nc.vector.tensor_tensor(hot[:, t], expert_no,
                                             idx_f[:, t, 0:TOPK].unsqueeze(2).to_broadcast([P, TOPK, NE]),
                                             ALU.is_equal))
                nc.vector.tensor_reduce(mask[:, t, :], hot[:, t].rearrange("p k e -> p e k"), AX.X,
                                        ALU.add).then_inc(mask_ok, 1)
            dve.wait_ge(ex_ok, T)
            link(nc.vector.reciprocal(einv, esum))
            for t in range(T):
                link(nc.vector.tensor_scalar(g4[:, t, :], ex4[:, t, :], einv[:, t:t + 1], None, ALU.mult))
                link(nc.vector.tensor_tensor(hotg[:, t], hot[:, t],
                                             g4[:, t, :].unsqueeze(2).to_broadcast([P, TOPK, NE]), ALU.mult))
                nc.vector.tensor_reduce(gate[:, t, :], hotg[:, t].rearrange("p k e -> p e k"), AX.X,
                                        ALU.add).then_inc(mask_ok, 1)
            dve.wait_ge(rank_ps, 1)
            link(nc.vector.tensor_reduce(cmax, ps[0:1, 1, 2 * NE:3 * NE], AX.X, ALU.max))
            link(nc.vector.tensor_scalar(rnd, cmax, float(CAP), 1.0, ALU.is_gt, ALU.add))
            for r in range(2, ROUNDS):
                link(nc.vector.tensor_scalar(rnd2, cmax, float(CAP * r), None, ALU.is_gt))
                link(nc.vector.tensor_tensor(rnd, rnd, rnd2, ALU.add))
            nc.vector.tensor_scalar(passes[:, :], rnd, float(NE), None, ALU.mult).then_inc(passes_ok, 1)
            link(nc.vector.scalar_tensor_tensor(out=ranked.rearrange("p t e -> p (t e)"), in0=ps[:, 1, 0:T * NE],
                                                scalar=FAR, in1=mask.rearrange("p t e -> p (t e)"),
                                                op0=ALU.add, op1=ALU.mult))
            dve.wait_ge(mask_ok, 2 * T)
            for r in range(ROUNDS):
                nc.vector.tensor_scalar(rank_col[:, :, r * NE:(r + 1) * NE], ranked, -FAR - CAP * r, None,
                                        ALU.add).then_inc(cols_ok, 1)
                nc.vector.tensor_copy(gate_col[:, :, r * NE:(r + 1) * NE], gate).then_inc(cols_ok, 1)
            dve.wait_ge(gateT_ps, 1)
            nc.vector.tensor_copy(gateT[:, :], ps[0:NE, 2, 0:TOK]).then_inc(gateT_ok, 1)

            dve.wait_ge(cols_ok, 2 * ROUNDS)
            for t in range(T):
                nc.vector.tensor_scalar(sel_next[:, t, :], slotno[:, 0:CAP], rank_col[:, t, 0:1], None,
                                        ALU.is_equal).then_inc(sel_ok, 1)
            gain2 = cst[:, C_G2:C_G2 + KD].unsqueeze(2).to_broadcast([P, KD, CAP])
            nc.vector.memset(sgT, 0.0).then_inc(sg_ok, 1)
            nc.vector.memset(out_sb, 0.0).then_inc(out_ok, 1)
            dve.wait_ge(xg_ps, 1)
            nc.vector.tensor_tensor(xgT, ps[:, 7, :].rearrange("p (k n) -> p k n", k=KD), gain2,
                                    ALU.mult).then_inc(xg_ok, 1)
            n_pass = dve.value_load(passes[0:1, 0:1], min_val=NE, max_val=NE * ROUNDS)
            with dve.Fori(0, n_pass) as n:
                n1 = dve.snap(n + 1)
                n2 = dve.snap(n + 2)
                e16 = dve.snap((n & (NE - 1)) * 16)
                dve.wait_ge(chunk_used[3], n1)
                nc.vector.tensor_copy(gu_sb[:, 0:BANK], ps[:, 4, :]).then_inc(gu_v, 1)
                for t in range(T):
                    nc.vector.tensor_scalar(sel_next[:, t, :], slotno[:, 0:CAP], rank_col[:, t, bass.ds(n1, 1)], None,
                                            ALU.is_equal).then_inc(sel_ok, 1)
                for t in range(T):
                    nc.vector.tensor_scalar(sel_gate[:, t, :], slotno, rank_col[:, t, bass.ds(n, 1)],
                                            gate_col[:, t, bass.ds(n, 1)], ALU.is_equal, ALU.mult).then_inc(sgate_ok, 1)
                dve.wait_ge(tp_ps, n1)
                nc.vector.tensor_tensor(gub.rearrange("p (j n) -> p j n", j=16),
                                        ps[:, 6:8, :].rearrange("p b (j n) -> p (b j) n", n=CAP),
                                        cst[:, bass.ds(e16 + C_BGU, 16)].unsqueeze(2).to_broadcast([P, 16, CAP]),
                                        ALU.add).then_inc(tp_read, 1)
                gv = gub.rearrange("p (j h n) -> p j h n", j=KD, h=2)
                as3 = lambda b: b.rearrange("p (j n) -> p j n", j=KD)
                dve.wait_ge(tp_read, n1)
                nc.vector.tensor_scalar(as3(g_cl), gv[:, :, 0, :], LIMIT, None, ALU.min).then_inc(g_ok, 1)
                nc.vector.tensor_scalar(as3(u_cl), gv[:, :, 1, :], LIMIT, -LIMIT, ALU.min, ALU.max).then_inc(u_ok, 1)
                dve.wait_ge(g_ok, n1)
                dve.wait_ge(u_ok, n1)
                nc.vector.scalar_tensor_tensor(out=act1, in0=u_cl, scalar=1.0, in1=g_cl, op0=ALU.add,
                                               op1=ALU.mult).then_inc(a1_ok, 1)
                dve.wait_ge(a1_ok, n1)
                dve.wait_ge(sig_ok, n1)
                nc.vector.tensor_tensor(actT, as3(act1), as3(sig), ALU.mult).then_inc(act_ok, 1)
                dve.wait_ge(xg_ps, n2)
                nc.vector.tensor_tensor(xgT, ps[:, 7, :].rearrange("p (k n) -> p k n", k=KD), gain2,
                                        ALU.mult).then_inc(xg_ok, 1)
                dve.wait_ge(sg_ps, n1)
                nc.vector.tensor_copy(sgT, ps[:, 4, 0:T * P].rearrange("p (t n) -> p t n", t=T)).then_inc(sg_ok, 1)

            dve.wait_ge(y_ok, 1)
            for n in range(2 * T):
                t, o = n // 2, (n % 2) * BANK
                nc.vector.tensor_tensor(x_sb[:, t, o:o + BANK], ps[:, n, :], x_sb[:, t, o:o + BANK],
                                        ALU.add).then_inc(x3_ok, 1)
            inverse_variance(2, sq_sum, D, 3 * T)
            dve.wait_ge(rstd_ok, 3)
            for t in range(T):
                nc.vector.scalar_tensor_tensor(out=x_sb[:, t, :], in0=x_sb[:, t, :], scalar=rstd[:, t:t + 1],
                                               in1=fin_g, op0=ALU.mult, op1=ALU.mult).then_inc(fin_ok, 1)

        @block.tensor
        def _(pe):
            def chunk_in(c):
                pe.wait_ge(slot_full[slot_of(c)], 16 * (use_of(c) + 1))

            def transposes(turn, tp0):
                pe.wait_ge(normed, T * (turn + 1))
                for k in range(KD):
                    for t in range(T):
                        o = (k % 2) * TOK + t * P
                        ins = nc.tensor.transpose(ps[:, tp0 + k // 2, o:o + P], hn[:, t, k::KD], ident)
                    ins.then_inc(tposed, 1)

            def group(i):
                c = {0: 0, 1: 1, 2: 4, 3: 5, 4: 6, 5: 7, 6: 8, 7: 9}[i // 4]
                w = ring[:, slot_of(c), :].rearrange("p (k n) -> p k n", k=KD)
                if i % 4 == 0:
                    chunk_in(c)
                if i >= 4:
                    pe.wait_ge(group_read, i // 2 * 2 - 2)
                for k in range(KD):
                    ins = nc.tensor.matmul(half(4 + (i // 2) % 2, i % 2), w[:, k, (i % 4) * P:(i % 4 + 1) * P],
                                           hT[:, k, :], start=(k == 0), stop=(k == KD - 1))
                ins.then_inc(group_done, 1)

            def lru_gate_products(u):
                w = ring[:, slot_of(3), 2048:4096].rearrange("p (m c n) -> p m c n", m=4, c=KD)
                for c in range(4 * u, 4 * u + 4):
                    pe.wait_ge(conv_ok, c + 1)
                    for m in range(4):
                        n = 4 * c + m
                        if n >= 4:
                            pe.wait_ge(gate_read, n // 2 * 2 - 2)
                        for r in range(2):
                            rs = slice(64 * r, 64 * r + 64)
                            ins = nc.tensor.matmul(ps[rs, 6 + (n % 4) // 2, (n % 2) * TOK:(n % 2 + 1) * TOK],
                                                   w[rs, m, c, :], xc[rs, c, :], start=True, stop=True)
                        ins.then_inc(gate_ps, 1)

            pe.wait_ge(sq_in, 16)
            transposes(0, 0)
            pe.wait_ge(hT_v, 2)
            pe.wait_ge(hT_a, 4)
            for i in range(8):
                group(i)
            for part in range(2):
                chunk_in(2 + part)
                n_col = QW if part == 0 else 2 * KVW
                w = ring[:, slot_of(2 + part), 0:KD * n_col].rearrange("p (k n) -> p k n", k=KD)
                for t in range(T):
                    for k in range(KD):
                        ins = nc.tensor.matmul(ps[:, 2 * t + part, 0:n_col], hT[:, k, t * P:(t + 1) * P], w[:, k, :],
                                               start=(k == 0), stop=(k == KD - 1))
                    ins.then_inc(qkv_done, 1)
            lru_gate_products(0)
            for i in range(8, 12):
                group(i)
            pe.wait_ge(rot_ok, T)
            kd = lru[:, 2, 0:T * NKV * P].rearrange("p (t g n) -> p t g n", t=T, g=NKV)
            for j in range(2):
                for jj in range(2):
                    for t in range(T):
                        a = 2 * j + jj
                        ins = nc.tensor.transpose(ps[:, j, jj * TOK + t * P:jj * TOK + (t + 1) * P],
                                                  qkv[:, t, a * P:(a + 1) * P], ident)
                ins.then_inc(qk_tp, 1)
            for g in range(NKV):
                for t in range(T):
                    ins = nc.tensor.transpose(ps[:, 2, g * TOK + t * P:g * TOK + (t + 1) * P], kd[:, t, g, :], ident)
            ins.then_inc(qk_tp, 1)
            for i in range(12, 16):
                group(i)
            lru_gate_products(1)

            def scores(h):
                rs = slice(64 * (h % 2), 64 * (h % 2) + 64)
                if h >= 2:
                    pe.wait_ge(exp_ok, T * (h - 1))
                for t in range(T):
                    ins = nc.tensor.matmul(ps[:, h % 2, t * TOK:(t + 1) * TOK], qT[rs, h // 2, t * P:(t + 1) * P],
                                           kT[rs, h // (NQ // NKV), :], start=True, stop=True)
                ins.then_inc(score_ps, 1)

            def prob_transposes(h):
                pe.wait_ge(prob_ok, T * (h + 1))
                if h >= 1:
                    pe.wait_ge(pT_ok, h)
                for kt in range(T):
                    for t in range(T):
                        ins = nc.tensor.transpose(ps[:, 2, kt * TOK + t * P:kt * TOK + (t + 1) * P],
                                                  prob[:, h % 2, t, kt * P:(kt + 1) * P], ident)
                ins.then_inc(pT_ps, 1)

            def values(h):
                g = h // (NQ // NKV)
                o = QW + KVW + g * HD
                pe.wait_ge(pT_ok, h + 1)
                if h >= 2:
                    pe.wait_ge(attn_ok, h // 2)
                for kt in range(T):
                    ins = nc.tensor.matmul(ps[64 * (h % 2):64 * (h % 2) + 64, 3, 0:TOK],
                                           qkv[:, kt, o:o + HD], probT[:, h % 2, kt, :],
                                           start=(kt == 0), stop=(kt == T - 1))
                ins.then_inc(pv_ps, 1)

            for i in range(16, 32):
                group(i)
                s = i - 20
                if s == 0:
                    pe.wait_ge(qk_cp, 3)
                if 0 <= s - 2 < NQ:
                    prob_transposes(s - 2)
                if 0 <= s < NQ:
                    scores(s)
                if 0 <= s - 3 < NQ:
                    values(s - 3)

            wA = ring[:, slot_of(10), :].rearrange("p (k n) -> p k n", k=4)
            wR = [ring[:, slot_of(11 + i), :].rearrange("p (k n) -> p k n", k=4) for i in range(2)]
            wO = [ring[:, slot_of(13 + i), :].rearrange("p (k n) -> p k n", k=4) for i in range(2)]

            def mix(c):
                if c % 4 == 0:
                    chunk_in(13 + c // 4)
                pe.wait_ge(merged_ok, c + 1)
                for n in range(2 * T):
                    t, o = n // 2, (n % 2) * BANK
                    ins = nc.tensor.matmul(ps[:, n, :], mergedT[:, c, t * P:(t + 1) * P], wO[c // 4][:, c % 4, o:o + BANK],
                                           start=(c == 0), stop=(c == KD - 1))
                if c % 4 == 3:
                    ins.then_inc(mixed_ps, 1)

            for g in range(KD):
                cols = slice(g * P, (g + 1) * P)
                if g == 0:
                    chunk_in(10)
                    chunk_in(11)
                    chunk_in(12)
                    pe.wait_ge(lru_unit, 2)
                    pe.wait_ge(attn_ok, 4)
                    pe.wait_ge(group_read, 32)
                if g >= 2:
                    pe.wait_ge(merged_ok, g - 1)
                for k in range(KD):
                    nc.tensor.matmul(half(4 + g % 2, 1), wR[k // 4][:, k % 4, cols], xc[:, k, :],
                                     start=(k == 0), stop=(k == KD - 1))
                for k in range(4):
                    ins = nc.tensor.matmul(half(4 + g % 2, 0), wA[:, k, cols], attnT[:, k, :],
                                           start=(k == 0), stop=(k == 3))
                ins.then_inc(branch_ps, 1)
                if g >= 1:
                    mix(g - 1)
            mix(KD - 1)

            transposes(1, 4)
            pe.wait_ge(hT_v, 4)
            pe.wait_ge(hT_a, 8)
            wr = cst[:, C_WR:C_WR + KD * NE].rearrange("p (k e) -> p k e", k=KD)
            for t in range(T):
                for k in range(KD):
                    ins = nc.tensor.matmul(ps[:, 0, t * NE:(t + 1) * NE], h2T[:, k, t * P:(t + 1) * P], wr[:, k, :],
                                           start=(k == 0), stop=(k == KD - 1))
            ins.then_inc(logit_ps, 1)
            pe.wait_ge(mask_ok, T)
            nc.tensor.matmul(ps[:, 1, 0:NE], upper, mask[:, 0, :], start=True, stop=True)
            nc.tensor.matmul(ps[:, 1, NE:2 * NE], ones, mask[:, 0, :], start=True, stop=False)
            nc.tensor.matmul(ps[:, 1, NE:2 * NE], upper, mask[:, 1, :], start=False, stop=True)
            for t in range(T):
                ins = nc.tensor.matmul(ps[:, 1, 2 * NE:3 * NE], ones, mask[:, t, :], start=(t == 0), stop=(t == T - 1))
            ins.then_inc(rank_ps, 1)
            pe.wait_ge(mask_ok, 2 * T)
            for t in range(T):
                ins = nc.tensor.transpose(ps[0:NE, 2, t * P:(t + 1) * P], gate[:, t, :], ident)
            ins.then_inc(gateT_ps, 1)

            def gather():
                for k in range(KD):
                    for t in range(T):
                        ins = nc.tensor.matmul(ps[:, 7, k * CAP:(k + 1) * CAP], hn[:, t, k::KD], sel_next[:, t, :],
                                               start=(t == 0), stop=(t == T - 1))
                return ins

            pe.wait_ge(gateT_ok, 1)
            pe.wait_ge(cols_ok, 2 * ROUNDS)
            pe.wait_ge(late_in, 48)
            for n in range(2 * T):
                t, o = n // 2, (n % 2) * BANK
                ins = nc.tensor.matmul(ps[:, n, :], gateT[:, t * P:(t + 1) * P], bdn[:, o:o + BANK],
                                       start=True, stop=False)
            ins.then_inc(ybias, 1)
            pe.wait_ge(sel_ok, T)
            gather().then_inc(xg_ps, 1)
            pe.wait_ge(ybias, 1)

            def scatter(last):
                for n in range(2 * T):
                    t, hf = n // 2, n % 2
                    rs = slice(64 * hf, 64 * hf + 64)
                    ins = nc.tensor.matmul(ps[:, n, :], sgT[rs, t, :], out_sb[rs, :], start=False, stop=last)
                return ins

            n_pass = pe.value_load(passes[0:1, 0:1], min_val=NE, max_val=NE * ROUNDS)
            with pe.Fori(0, n_pass) as n:
                n1 = pe.snap(n + 1)
                n2 = pe.snap(n + 2)
                sel_n = pe.snap(n * T + 2 * T)
                sgate_n = pe.snap(n * T + T)
                full = {u: pe.snap(n * 16 + 16 * (u + 1)) for u in sorted({u for _, u in EXP})}
                pe.wait_ge(xg_ok, n1)
                pe.wait_ge(sg_ok, n1)
                for j in range(4):
                    s, u = EXP[j]
                    pe.wait_ge(slot_full[s], full[u])
                    w = ring[:, s, :].rearrange("p (r n) -> p r n", r=2)
                    for r in range(2):
                        k = 2 * j + r
                        for b in range(2):
                            for side in range(2):
                                o = side * FF + b * BANK
                                ins = nc.tensor.matmul(ps[64 * side:64 * side + 64, 4 + b, :], xgT[:, k, :],
                                                       w[:, r, o:o + BANK], start=(k == 0), stop=(k == KD - 1))
                    ins.then_inc(chunk_used[j], 1)
                pe.wait_ge(out_ok, n1)
                scatter(False)
                pe.wait_ge(gu_v, n1)
                pe.wait_ge(gu_a, n1)
                for j in range(KD):
                    o = (j % 4) * P
                    ins = nc.tensor.transpose(ps[:, 6 + j // 4, o:o + P], gu_sb[:, j::KD], ident)
                ins.then_inc(tp_ps, 1)
                pe.wait_ge(sel_ok, sel_n)
                pe.wait_ge(tp_read, n1)
                gather().then_inc(xg_ps, 1)
                pe.wait_ge(sgate_ok, sgate_n)
                for t in range(T):
                    ins = nc.tensor.transpose(ps[:, 4, t * P:(t + 1) * P], sel_gate[:, t, :], ident)
                ins.then_inc(sg_ps, 1)
                pe.wait_ge(act_ok, n1)
                for j in range(2):
                    s, u = EXP[4 + j]
                    pe.wait_ge(slot_full[s], full[u])
                    w = ring[:, s, :].rearrange("p (r n) -> p r n", r=4)
                    for r in range(4):
                        k = 4 * j + r
                        for side in range(2):
                            ins = nc.tensor.matmul(ps[64 * side:64 * side + 64, 6, :], actT[:, k, :],
                                                   w[:, r, side * BANK:(side + 1) * BANK],
                                                   start=(k == 0), stop=(k == KD - 1))
                    ins.then_inc(chunk_used[4 + j], 1)
            last = pe.snap(n_pass + 1)
            pe.wait_ge(out_ok, last)
            pe.wait_ge(sg_ok, last)
            scatter(True).then_inc(y_ok, 1)


def _layouts(a):
    w_in = a["w_in"][0].reshape(P, KD, -1)
    o = QKV
    parts = [w_in[:, :, o:o + 512], w_in[:, :, o + 512:o + 1024], w_in[:, :, 0:QW]]
    blocks = lambda w: w.reshape(2, KD, 2, 64, 64).transpose(2, 3, 0, 1, 4).reshape(P, 2, KD, 64)
    wa, wi = blocks(a["lru_wa"][0]), blocks(a["lru_wi"][0])
    gates = np.stack([wa[:, 0], wi[:, 0], wa[:, 1], wi[:, 1]], axis=1)
    kv = np.concatenate([w_in[:, :, QW:QKV].reshape(P, -1), gates.reshape(P, -1)], axis=1)
    rest = [w_in[:, :, o + 1024 + 512 * i:o + 1536 + 512 * i] for i in range(6)]
    rows4 = lambda w: [w.reshape(-1, 4, P, D)[i].transpose(1, 0, 2) for i in range(w.shape[0] // 512)]
    chunks = parts + [kv] + rest + rows4(a["w_attn_o"][0]) + rows4(a["w_lru_o"][0]) + rows4(a["w_out"][0])
    pre = np.stack([np.ascontiguousarray(c).reshape(P, CH) for c in chunks])

    chan = lambda v: v.reshape(-1, P).T
    rows = TOK // GRID_W
    f32 = np.float32
    inv = THETA ** (-np.arange(0, HD // 2, 2, dtype=f32) / (HD // 2))
    row = np.repeat(np.arange(rows), GRID_W).astype(f32)
    colm = np.tile(np.arange(GRID_W), rows).astype(f32)
    ang_r, ang_c = row[:, None] * inv[None], colm[:, None] * inv[None]
    cos = np.concatenate([np.cos(ang_r)] * 2 + [np.cos(ang_c)] * 2, axis=1).astype(f32)
    sin = np.concatenate([-np.sin(ang_r), np.sin(ang_r), -np.sin(ang_c), np.sin(ang_c)], axis=1).astype(f32)
    tiles = lambda t: t.reshape(T, P, HD).transpose(1, 0, 2).reshape(P, -1)
    lb = np.concatenate([chan(a[k][0, d]) for d in range(2) for k in ("lru_ba", "lru_bi")], axis=1)
    bgu = a["b_gu"][0].reshape(NE, 2, P, KD).transpose(2, 0, 3, 1).reshape(P, -1)
    wr = a["w_router"][0].reshape(P, KD * NE)
    consts = np.concatenate([
        a["norm1_g"][0].reshape(P, KD), a["norm2_g"][0].reshape(P, KD), chan(a["b_in"][0][QKV:]),
        *[chan(a["conv_w"][0, j]) for j in range(TAPS)], chan(a["conv_b"][0]), lb,
        chan(a["lru_lambda"][0, 0]), chan(a["lru_lambda"][0, 1]), tiles(cos), tiles(sin), bgu, wr], axis=1)
    squares = np.stack([np.eye(P), np.triu(np.ones((P, P)), 1), np.ones((P, P)),
                        np.tile(np.arange(CAP), (P, P // CAP))], axis=1).astype(f32)
    one_row = np.concatenate([a["b_in"][0][:QKV], a["q_norm_g"][0], a["k_norm_g"][0], a["b_router"][0],
                              a["final_g"]])[None]
    return {"x": a["x"].reshape(TOK, D), "consts": consts, "squares": squares, "rows": one_row, "pre": pre,
            "w_gu": a["w_gu"][0], "w_down": a["w_down"][0], "b_down": a["b_down"][0]}


def kernel(**inputs):
    import concourse.bacc as _bacc
    from concourse.bass_utils import run_bass_kernel_spmd as _run

    arrays = _layouts({k: np.asarray(v) for k, v in inputs.items()})
    nc = _bacc.Bacc("TRN2", target_bir_lowering=False, num_devices=1, dynamic_dma_scratch_size=1024)
    feed, args = {}, []
    for name, a in arrays.items():
        a = np.ascontiguousarray(a)
        feed[f"in_{name}_dram"] = a
        args.append(nc.dram_tensor(f"in_{name}_dram", a.shape, mybir.dt.from_np(a.dtype), kind="ExternalInput").ap())
    args.append(nc.dram_tensor("out_0_dram", (TOK, D), mybir.dt.float32, kind="ExternalOutput").ap())
    encoder_layer(nc, *args)
    r = _run(nc, [feed], core_ids=[0])
    return r.results[0]["out_0_dram"].reshape(1, TOK, D)
```

```python
import numpy as np
import concourse.bass as bass
from concourse import mybir
from contextlib import ExitStack

P = 128
D = 1024
TOK = 256
T = TOK // P
KD = D // P
HD = 64
NQ, NKV = 8, 2
NH = NQ + NKV
QW, KVW = NQ * HD, NKV * HD
QKV = QW + 2 * KVW
GRID_W = 64
THETA = 10000.0
EPS = 1e-6
RG_C = 8.0
TAPS, PAD_L, PAD_R = 4, 1, 2
NE, TOPK = 32, 4
FF = 1024
LIMIT, ALPHA = 7.0, 1.702
BANK = 512
CH = 4096
SLOTS = 8
PSLOTS = 7
PRE = 16
PER = 6
UNROLL = 4
CAP = 64
ROUNDS = TOK // CAP
FAR = 4096.0

C_G1, C_G2, C_BIN, C_CW, C_CB, C_LB, C_LAM, C_COS, C_SIN, C_BGU, C_WR = (
    0, 8, 16, 48, 80, 88, 120, 136, 264, 392, 904)
C_ALL = C_WR + KD * NE


def encoder_layer(nc, x, consts, squares, rows, pre, w_gu, w_down, b_down, out):
    f32, i32, u32 = mybir.dt.float32, mybir.dt.int32, mybir.dt.uint32
    ALU, ACT, AX = mybir.AluOpType, mybir.ActivationFunctionType, mybir.AxisListType

    ctx = ExitStack()
    with ctx:
        def sb(name, shape, dt=f32):
            return ctx.enter_context(nc.sbuf_tensor(name, shape, dt))

        def sem(name):
            return ctx.enter_context(nc.semaphore(name))

        ring = sb("ring", [P, PSLOTS, CH])
        wide = sb("wide", [P, CH])
        hT = wide[:, 0:KD * TOK].rearrange("p (k n) -> p k n", k=KD)
        xc = wide[:, KD * TOK:].rearrange("p (k n) -> p k n", k=KD)
        x_sb = sb("x_sb", [P, T, D])
        hn = sb("hn", [P, T, D])
        MARGIN = PAD_L + TOK + PAD_R
        xr_flat = sb("xr_flat", [P, KD * MARGIN])
        xr = xr_flat[:, :].rearrange("p (k n) -> p k n", k=KD)
        gR = xr_flat[:, 0:KD * TOK].rearrange("p (k n) -> p k n", k=KD)
        gelu = sb("gelu", [P, KD, TOK])
        lru = sb("lru", [P, 4 * 2048])
        qkv = sb("qkv", [P, T, QKV])
        qT = sb("qT", [P, NQ // 2, TOK])
        attnT = qT
        kT = sb("kT", [P, NKV, TOK])
        pbuf = sb("pbuf", [P, 4 * T * TOK])
        prob = pbuf[:, 0:2 * T * TOK].rearrange("p (a t n) -> p a t n", a=2, t=T)
        probT = pbuf[:, 2 * T * TOK:].rearrange("p (a t n) -> p a t n", a=2, t=T)
        bqkv, gains = pbuf[:, 0:QKV], pbuf[:, QKV:QKV + NH * HD]
        k_twice = pbuf[:, QKV + NH * HD:QKV + NH * HD + T * NKV * P]
        cst = sb("cst", [P, C_ALL])
        sq = sb("sq", [P, 4, P])
        brt = sb("brt", [P, NE])
        small = sb("small", [P, 256])

        ident, upper, ones, slotno = (sq[:, i, :] for i in range(4))
        hb = cst[:, C_BIN + 16:C_BIN + 32]
        gA = hn[:, :, :].rearrange("p t d -> p (t d)").rearrange("p (k n) -> p k n", k=KD)

        col = [0]

        def scratch(n):
            col[0] += n
            return small[:, col[0] - n:col[0]]

        ssum, rstd = scratch(2), scratch(2)
        qk_rstd = scratch(T * NH)
        lam_h, lam_f = scratch(16), scratch(16)
        warm = scratch(1)
        lam_t = [scratch(16) for _ in range(4)]
        neg_max, exp_sum = scratch(4), scratch(4)

        lruR, lruI, lruA, lruE = (lru[:, 2048 * i:2048 * (i + 1)] for i in range(4))
        mergedT = lruR.rearrange("p (k n) -> p k n", k=KD)
        x2T = lruI.rearrange("p (k n) -> p k n", k=KD)
        m_a, m_r = lruA[:, 0:512], lruA[:, 512:1024]
        at = [0]

        def part(n):
            at[0] += n
            return lru[:, at[0] - n:at[0]]

        gu_sb, gub = part(2 * BANK), part(2 * BANK)
        xgT = part(KD * CAP).rearrange("p (k n) -> p k n", k=KD)
        g_cl, sig, act1, u_cl = (part(KD * CAP) for _ in range(4))
        actT = part(KD * CAP).rearrange("p (k n) -> p k n", k=KD)
        pair_out = [part(D) for _ in range(2)]
        sel_next = part(T * CAP).rearrange("p (t n) -> p t n", t=T)
        sel_gate = part(T * P).rearrange("p (t n) -> p t n", t=T)
        sgT = [part(T * P).rearrange("p (t n) -> p t n", t=T) for _ in range(2)]
        NCOL = (ROUNDS + 1) * NE
        pflat, tflat = pbuf[:, 0:1024], pbuf[:, 1024:2048]
        rank_col = pflat[:, 0:T * NCOL].rearrange("p (t n) -> p t n", t=T)
        gate_col = pflat[:, T * NCOL:2 * T * NCOL].rearrange("p (t n) -> p t n", t=T)
        logit = tflat[:, 0:64].rearrange("p (t e) -> p t e", t=T)
        top8 = tflat[:, 64:80].rearrange("p (t k) -> p t k", t=T)
        idx_f = tflat[:, 80:96].rearrange("p (t k) -> p t k", t=T)
        ex4 = tflat[:, 96:104].rearrange("p (t k) -> p t k", t=T)
        g4 = tflat[:, 104:112].rearrange("p (t k) -> p t k", t=T)
        nmax, esum, einv = tflat[:, 112:114], tflat[:, 114:116], tflat[:, 116:118]
        hot = tflat[:, 128:384].rearrange("p (t k e) -> p t k e", t=T, k=TOPK)
        hotg = tflat[:, 384:640].rearrange("p (t k e) -> p t k e", t=T, k=TOPK)
        mask = tflat[:, 640:704].rearrange("p (t e) -> p t e", t=T)
        gate = tflat[:, 704:768].rearrange("p (t e) -> p t e", t=T)
        ranked = tflat[:, 768:832].rearrange("p (t e) -> p t e", t=T)
        wrg = qkv[:, 0, 0:KD * NE].rearrange("p (k e) -> p k e", k=KD)
        gateT = qkv[0:NE, 1, 0:TOK]
        cmax, rnd, rnd2 = tflat[0:1, 832:833], tflat[0:1, 833:834], tflat[0:1, 834:835]
        idx_u = sb("idx_u", [P, T, 8], u32)
        passes = sb("passes", [1, 1], i32)
        fin_g = gelu[:, 0:4, :].rearrange("p k n -> p (k n)")
        bdn = gelu[0:NE, 4:8, :].rearrange("p k n -> p (k n)")

        ps = ctx.enter_context(nc.psum_tensor("ps", [P, 8, BANK], f32))

        def half(bank, h):
            return ps[:, bank, h * TOK:(h + 1) * TOK]

        x_in, cst_in, sq_in, bias_in, late_in, out_done_dma = (
            sem(n) for n in ("x_in", "cst_in", "sq_in", "bias_in", "late_in", "out_stored"))
        slot_full = [sem(f"slot_full{i}") for i in range(SLOTS)]
        chunk_used = [sem(f"chunk_used{j}") for j in range(SLOTS)]
        v_step, a_step = sem("v_step"), sem("a_step")
        sq_sum, var_inv, rstd_ok, normed = sem("sq_sum"), sem("var_inv"), sem("rstd_ok"), sem("normed")
        tposed, hT_v, hT_a = sem("tposed"), sem("hT_v"), sem("hT_a")
        group_done, group_read = sem("group_done"), sem("group_read")
        qkv_done, qkv_ok = sem("qkv_done"), sem("qkv_ok")
        conv_ok, conv_half = sem("conv_ok"), sem("conv_half")
        margins = sem("margins")
        gate_ps, gate_read, lru_x, lru_t, lru_w, lru_s, lru_unit = (
            sem(n) for n in ("lru_gate_ps", "lru_gate_read", "lru_exp", "lru_t", "lru_w", "lru_s", "lru_unit"))
        gelu_ok, xT_v, xT_a, wrg_ok, warm_ok = (
            sem(n) for n in ("gelu_ok", "x2T_v", "x2T_a", "router_weights_ok", "warm_ok"))
        lam_e, lam_ok, hb_ok = sem("lam_exp"), sem("lam_ok"), sem("half_bias_ok")
        qk_inv, qk_rs, rot_ok, qk_tp, qk_cp = sem("qk_inv"), sem("qk_rs"), sem("rot_ok"), sem("qk_tposed"), sem("qk_copied")
        score_ps, max_ok, exp_ok, prob_ok, pT_ps, pT_ok, pv_ps, attn_ok = (
            sem(n) for n in ("score_ps", "max_ok", "exp_ok", "prob_ok", "probT_ps", "probT_ok", "pv_ps", "attn_ok"))
        branch_ps, merged_ok, mixed_ps, x2_ok = sem("branch_ps"), sem("merged_ok"), sem("mixed"), sem("x2_ok")
        logit_ps, top_ok, ex_ok, mask_ok, rank_ps, gateT_ps, gateT_ok, cols_ok, passes_ok, ybias = (
            sem(n) for n in ("logit_ps", "top_ok", "top_exp_ok", "mask_ok", "rank_ps", "gateT_ps", "gateT_ok",
                             "cols_ok", "passes_ok", "y_bias"))
        sel_ok, xg_ps, xg_ok, gu_v, gu_a, tp_ps, tp_read, sgate_ok, sg_ps, sg_ok = (
            sem(n) for n in ("sel_ok", "xg_ps", "xg_ok", "gu_copied_v", "gu_copied_a", "tp_ps", "tp_read",
                             "sel_gate_ok", "sgT_ps", "sgT_ok"))
        g_ok, sig_ok, u_ok, a1_ok, act_ok, out_ok, y_ok = (
            sem(n) for n in ("g_clamped", "sigmoid_ok", "u_clamped", "gated_ok", "act_ok", "out_ok", "y_ok"))
        x3_ok, fin_ok = sem("x3_ok"), sem("fin_ok")

        block = ctx.enter_context(nc.Block())

        gu_chunk = w_gu.rearrange("e (p j r) n -> e j p (r n)", j=4, r=2)
        dn_chunk = w_down.rearrange("e (p j r) n -> e j p (r n)", j=2, r=4)

        SLOT_ORDER = [(PRE + i) % PSLOTS for i in range(SLOTS - 3)] + [PSLOTS, 0, 1]
        EARLIER = [len(range(s, PRE, PSLOTS)) if s < PSLOTS else 0 for s in range(SLOTS)]

        def slot(s):
            return ring[:, s, :] if s < PSLOTS else wide[:, :]

        def slot_of(chunk):
            return chunk % PSLOTS

        def use_of(chunk):
            return chunk // PSLOTS

        CONSUMED = ([(group_done, 4), (group_done, 8), (qkv_done, T), (qkv_done, 2 * T), (gate_ps, 32)]
                    + [(group_done, 12 + 4 * i) for i in range(6)]
                    + [(branch_ps, KD)] * 3 + [(mixed_ps, 1), (mixed_ps, 2)])

        def expert_src(e, j):
            c = gu_chunk[e, j] if j < 4 else dn_chunk[e, j - 4]
            return c if isinstance(e, int) else c.rearrange("o p n -> (o p) n")

        @block.sync
        def _(sp):
            for t in range(T):
                sp.dma_start(x_sb[:, t, :], x[t * P:(t + 1) * P, :]).then_inc(x_in, 16)
            for c in range(PRE):
                if c >= PSLOTS:
                    sp.wait_ge(*CONSUMED[c - PSLOTS])
                sp.dma_start(slot(slot_of(c)), pre[c, :, :]).then_inc(slot_full[slot_of(c)], 16)
            for k in range(UNROLL * PER):
                s = SLOT_ORDER[k % SLOTS]
                if s == PSLOTS and k < SLOTS:
                    sp.wait_ge(branch_ps, KD)
                elif k < SLOTS:
                    sp.wait_ge(*CONSUMED[(PRE - 1) - (PRE - 1 - s) % PSLOTS])
                else:
                    sp.wait_ge(chunk_used[(k - SLOTS) % PER], (k - SLOTS) // PER + 1)
                sp.dma_start(slot(s), expert_src(k // PER, k % PER)).then_inc(slot_full[s], 16)
            sp.wait_ge(passes_ok, 1)
            n_pass = sp.value_load(passes[0:1, 0:1], min_val=NE, max_val=NE * ROUNDS)
            with sp.Fori(UNROLL, n_pass, UNROLL) as n:
                for i in range(UNROLL):
                    e = sp.snap(sp.to_reg((n + i) & (NE - 1)), min_val=0, max_val=NE - 1)
                    used = {q: sp.snap(n + q) for q in sorted({(PER * i + j - SLOTS) // PER + 1 for j in range(PER)})}
                    for j in range(PER):
                        k = PER * i + j
                        s = SLOT_ORDER[k % SLOTS]
                        sp.wait_ge(chunk_used[(k - SLOTS) % PER], used[(k - SLOTS) // PER + 1])
                        sp.dma_start(slot(s), expert_src(bass.ds(e, 1), j)).then_inc(slot_full[s], 16)
            for t in range(T):
                sp.wait_ge(fin_ok, t + 1)
                sp.dma_start(out[t * P:(t + 1) * P, :], x_sb[:, t, :]).then_inc(out_done_dma, 16)
            sp.wait_ge(out_done_dma, 16 * T)

        @block.scalar
        def _(act):
            act.dma_start(sq[:, :, :], squares).then_inc(sq_in, 16)
            act.dma_start(cst[:, :], consts).then_inc(cst_in, 16)
            act.dma_start(bqkv[:, :], rows[0:1, 0:QKV].to_broadcast([P, QKV])).then_inc(bias_in, 16)
            for h in range(NH):
                o = QKV + (0 if h < NQ else HD)
                act.dma_start(gains[:, h * HD:(h + 1) * HD], rows[0:1, o:o + HD].to_broadcast([P, HD])).then_inc(bias_in, 16)
            o = QKV + 2 * HD
            act.dma_start(brt[:, :], rows[0:1, o:o + NE].to_broadcast([P, NE])).then_inc(late_in, 16)

            def norm_rows(turn, ready, value):
                for t in range(T):
                    act.wait_ge(ready, value(t))
                    dst = (hn[:, t, :], lruE[:, t * D:(t + 1) * D], lruA[:, t * D:(t + 1) * D])[turn]
                    nc.scalar.activation(dst, x_sb[:, t, :], ACT.Square,
                                         accum_out=ssum[:, t:t + 1]).then_inc(sq_sum, 1)
                act.wait_ge(var_inv, turn + 1)
                nc.scalar.activation(rstd, ssum, ACT.Sqrt).then_inc(rstd_ok, 1)

            def load_sqrt_table(times):
                act.wait_ge(warm_ok, times)
                nc.scalar.activation(warm, warm, ACT.Sqrt).then_inc(warm_ok, 1)

            def scaled_copy(g, dst, tp0):
                for k in range(4, 8):
                    act.wait_ge(tposed, k // 2 * 2 + 2)
                    nc.scalar.activation(dst[:, k, :], half(tp0 + k // 2, k % 2), ACT.Copy,
                                         scale=cst[:, g + k:g + k + 1]).then_inc(hT_a, 1)

            def group(i):
                act.wait_ge(group_done, i // 2 * 2 + 2)
                src = half(4 + (i // 2) % 2, i % 2)
                if i < 8:
                    if i == 0:
                        act.wait_ge(margins, 1)
                        act.wait_ge(hb_ok, 2)
                    nc.scalar.activation(xr[:, i, PAD_L:PAD_L + TOK], src, ACT.Identity,
                                         bias=cst[:, C_BIN + i:C_BIN + i + 1]).then_inc(group_read, 1)
                elif i < 16:
                    nc.scalar.activation(gelu[:, i - 8, :], src, ACT.Identity,
                                         bias=cst[:, C_BIN + i:C_BIN + i + 1]).then_inc(group_read, 1)
                else:
                    dst = gA[:, i - 16, :] if i < 24 else gR[:, i - 24, :]
                    if i == 24:
                        act.wait_ge(conv_ok, KD)
                    nc.scalar.activation(dst, src, ACT.Tanh, scale=0.5,
                                         bias=hb[:, i - 16:i - 15]).then_inc(group_read, 1)

            def lru_gates(u):
                if u == 1:
                    act.wait_ge(lru_unit, 1)
                for c in range(4):
                    for m in range(4):
                        n = 16 * u + 4 * c + m
                        act.wait_ge(gate_ps, n // 2 * 2 + 2)
                        dst = (lruR if m % 2 == 0 else lruI)[:, (m // 2 * 4 + c) * TOK:(m // 2 * 4 + c + 1) * TOK]
                        b = C_LB + m * 8 + 4 * u + c
                        nc.scalar.activation(dst, half(6 + (n % 4) // 2, n % 2), ACT.Tanh, scale=0.5,
                                             bias=cst[:, b:b + 1]).then_inc(gate_read, 1)

            def lru_decay(u):
                act.wait_ge(gate_read, 16 * (u + 1))
                act.wait_ge(lam_ok, 1)
                if u == 0:
                    act.wait_ge(rot_ok, T)
                blocks = [((4 * d + c) * TOK, 8 * d + 4 * u + c) for d in range(2) for c in range(4)]
                for dst, lam in ((lruA, lam_h), (lruE, lam_f)):
                    for o, k in blocks:
                        nc.scalar.activation(dst[:, o:o + TOK], lruR[:, o:o + TOK], ACT.Exp, scale=lam[:, k:k + 1],
                                             bias=lam[:, k:k + 1]).then_inc(lru_x, 1)
                act.wait_ge(lru_x, 16 * (u + 1))
                for o, k in blocks:
                    nc.scalar.activation(lruR[:, o:o + TOK], lruR[:, o:o + TOK], ACT.Tanh, scale=lam_h[:, k:k + 1],
                                         bias=lam_h[:, k:k + 1]).then_inc(lru_t, 1)

            def lru_root(u):
                act.wait_ge(lru_w, u + 1)
                nc.scalar.activation(lruE, lruE, ACT.Sqrt, scale=-0.25).then_inc(lru_s, 1)

            load_sqrt_table(1)
            norm_rows(0, x_in, lambda t: 16 * T)
            act.wait_ge(cst_in, 16)
            scaled_copy(C_G1, hT, 0)
            act.wait_ge(lam_e, 1)
            nc.scalar.activation(lam_t[1], lam_t[0], ACT.Exp, scale=-1.0).then_inc(lam_e, 1)
            for i in range(8):
                group(i)
            act.wait_ge(qk_inv, 1)
            nc.scalar.activation(qk_rstd, qk_rstd, ACT.Sqrt).then_inc(qk_rs, 1)
            lru_gates(0)
            for i in range(8, 10):
                group(i)
            lru_decay(0)
            for i in range(10, 12):
                group(i)
            lru_root(0)
            for j in range(2):
                act.wait_ge(qk_tp, j + 1)
                nc.scalar.activation(qT[:, 2 * j:2 * j + 2, :].rearrange("p a n -> p (a n)"), ps[:, j, :],
                                     ACT.Copy).then_inc(qk_cp, 1)
            act.wait_ge(qk_tp, 3)
            nc.scalar.activation(kT[:, :, :].rearrange("p a n -> p (a n)"), ps[:, 2, :], ACT.Copy).then_inc(qk_cp, 1)
            for i in range(12, 16):
                group(i)
            act.wait_ge(group_read, 16)
            gelu_all = gelu[:, :, :].rearrange("p k n -> p (k n)")
            nc.scalar.activation(gelu_all, gelu_all, ACT.Gelu_apprx_tanh).then_inc(gelu_ok, 1)
            lru_gates(1)
            for i in range(16, 32):
                if i == 18:
                    lru_decay(1)
                if i == 20:
                    lru_root(1)
                group(i)
                s = i - 21
                if 0 <= s - 2 < NQ:
                    h = s - 2
                    act.wait_ge(pT_ps, h + 1)
                    nc.scalar.activation(probT[:, h % 2, :, :].rearrange("p a n -> p (a n)"), ps[:, 2, :],
                                         ACT.Copy).then_inc(pT_ok, 1)
                if 0 <= s < NQ:
                    act.wait_ge(max_ok, s + 1)
                    for t in range(T):
                        b = (s % 2) * T + t
                        nc.scalar.activation(prob[:, s % 2, t, :], ps[:, s % 2, t * TOK:(t + 1) * TOK], ACT.Exp,
                                             bias=neg_max[:, b:b + 1], scale=HD ** -0.5,
                                             accum_out=exp_sum[:, b:b + 1]).then_inc(exp_ok, 1)
            load_sqrt_table(2)
            act.wait_ge(lru_unit, 3)
            act.dma_start(fin_g, rows[0:1, o + NE:o + NE + D].to_broadcast([P, D])).then_inc(late_in, 16)
            act.dma_start(bdn, b_down).then_inc(late_in, 16)
            norm_rows(1, x2_ok, lambda t: 2 * t + 2)
            for b in range(2, 4):
                act.wait_ge(tposed, 8 + 2 * b + 2)
                nc.scalar.activation(x2T[:, 2 * b:2 * b + 2, :].rearrange("p k n -> p (k n)"), ps[:, 4 + b, :],
                                     ACT.Copy).then_inc(xT_a, 1)
            act.wait_ge(rstd_ok, 2)
            for t in range(T):
                nc.scalar.activation(hn[:, t, :], x_sb[:, t, :], ACT.Copy, scale=rstd[:, t:t + 1]).then_inc(normed, 1)
            for t in range(T):
                act.wait_ge(top_ok, 1)
                nc.scalar.activation(ex4[:, t, :], top8[:, t, 0:TOPK], ACT.Exp, bias=nmax[:, t:t + 1],
                                     accum_out=esum[:, t:t + 1]).then_inc(ex_ok, 1)

            act.wait_ge(passes_ok, 1)
            n_pass = act.value_load(passes[0:1, 0:1], min_val=NE, max_val=NE * ROUNDS)
            with act.Fori(0, n_pass, UNROLL) as n:
                for i in range(UNROLL):
                    n1 = act.snap(n + i + 1)
                    act.wait_ge(chunk_used[3], n1)
                    nc.scalar.activation(gu_sb[:, BANK:2 * BANK], ps[:, 5, :], ACT.Copy).then_inc(gu_a, 1)
                    act.wait_ge(g_ok, n1)
                    nc.scalar.activation(sig, g_cl, ACT.Sigmoid, scale=ALPHA).then_inc(sig_ok, 1)
                    act.wait_ge(chunk_used[5], n1)
                    rs = slice(64 * (i % 2), 64 * (i % 2) + 64)
                    for side in range(2):
                        nc.scalar.activation(pair_out[i // 2][rs, side * BANK:(side + 1) * BANK],
                                             ps[64 * side:64 * side + 64, 6, :], ACT.Copy).then_inc(out_ok, 1)

            load_sqrt_table(3)
            norm_rows(2, x3_ok, lambda t: 2 * t + 2)

        @block.vector
        def _(dve):
            steps = [0]

            def link(ins):
                steps[0] += 1
                ins.then_inc(v_step, 1)
                dve.wait_ge(v_step, steps[0])

            def inverse_variance(turn, total, n, value):
                dve.wait_ge(total, value)
                link(nc.vector.tensor_scalar(ssum, ssum, 1.0 / n, EPS, ALU.mult, ALU.add))
                nc.vector.reciprocal(ssum, ssum).then_inc(var_inv, 1)

            def norm_apply():
                dve.wait_ge(rstd_ok, 1)
                for t in range(T):
                    nc.vector.tensor_scalar(hn[:, t, :], x_sb[:, t, :], rstd[:, t:t + 1], None,
                                            ALU.mult).then_inc(normed, 1)

            def scaled_copy(g, dst, tp0):
                for b in range(2):
                    dve.wait_ge(tposed, 2 * b + 2)
                    nc.vector.tensor_tensor(
                        dst[:, 2 * b:2 * b + 2, :], ps[:, tp0 + b, :].rearrange("p (k n) -> p k n", k=2),
                        cst[:, g + 2 * b:g + 2 * b + 2].unsqueeze(2).to_broadcast([P, 2, TOK]),
                        ALU.mult).then_inc(hT_v, 1)

            nc.vector.memset(warm, 1.0).then_inc(warm_ok, 1)
            nc.vector.memset(xr[:, :, 0:PAD_L], 0.0)
            nc.vector.memset(xr[:, :, PAD_L + TOK:], 0.0).then_inc(margins, 1)
            dve.wait_ge(cst_in, 16)
            nc.vector.tensor_scalar(hb, hb, 0.5, None, ALU.mult).then_inc(hb_ok, 1)
            nc.vector.tensor_scalar(cst[:, C_LB:C_LB + 32], cst[:, C_LB:C_LB + 32], 0.5, None,
                                    ALU.mult).then_inc(hb_ok, 1)
            inverse_variance(0, sq_sum, D, T)
            norm_apply()
            scaled_copy(C_G1, hT, 0)

            lam = cst[:, C_LAM:C_LAM + 16]
            link(nc.vector.tensor_scalar(lam_t[0], lam, -1.0, None, ALU.mult))
            nc.vector.tensor_tensor(lam_t[0], lam_t[0], lam, ALU.max).then_inc(lam_e, 1)
            dve.wait_ge(lam_e, 2)
            link(nc.vector.tensor_scalar(lam_t[2], lam_t[1], 2.0, None, ALU.add))
            link(nc.vector.reciprocal(lam_t[2], lam_t[2]))
            link(nc.vector.tensor_tensor(lam_t[1], lam_t[1], lam_t[2], ALU.mult))
            link(nc.vector.tensor_tensor(lam_t[2], lam_t[1], lam_t[1], ALU.mult))
            link(nc.vector.tensor_scalar(lam_t[3], lam_t[2], 1.0 / 17, 1.0 / 15, ALU.mult, ALU.add))
            for q in (13, 11, 9, 7, 5, 3, 1):
                link(nc.vector.tensor_tensor(lam_t[3], lam_t[3], lam_t[2], ALU.mult))
                link(nc.vector.tensor_scalar(lam_t[3], lam_t[3], 1.0 / q, None, ALU.add))
            link(nc.vector.tensor_tensor(lam_t[3], lam_t[3], lam_t[1], ALU.mult))
            link(nc.vector.tensor_scalar(lam_t[0], lam, 0.0, RG_C, ALU.min, ALU.mult))
            link(nc.vector.tensor_scalar(lam_t[3], lam_t[3], 2 * RG_C, None, ALU.mult))
            link(nc.vector.tensor_tensor(lam_f, lam_t[0], lam_t[3], ALU.subtract))
            nc.vector.tensor_scalar(lam_h, lam_f, 0.5, None, ALU.mult).then_inc(lam_ok, 1)

            for c in range(KD):
                dve.wait_ge(group_read, c + 1)
                w = [cst[:, C_CW + 8 * j + c:C_CW + 8 * j + c + 1] for j in range(TAPS)]
                b = cst[:, C_CB + c:C_CB + c + 1]
                link(nc.vector.tensor_scalar(xc[:, c, :], xr[:, c, 0:TOK], w[0], b, ALU.mult, ALU.add))
                for j in range(1, TAPS):
                    ins = nc.vector.scalar_tensor_tensor(out=xc[:, c, :], in0=xr[:, c, j:j + TOK], scalar=w[j],
                                                         in1=xc[:, c, :], op0=ALU.mult, op1=ALU.add)
                    if j < TAPS - 1:
                        link(ins)
                    else:
                        ins.then_inc(conv_ok, 1)

            dve.wait_ge(bias_in, 16 * (1 + NH))
            for n in range(2 * T):
                part, t = n // T, n % T
                dve.wait_ge(qkv_done, n + 1)
                w = QW if part == 0 else 2 * KVW
                o = 0 if part == 0 else QW
                nc.vector.tensor_tensor(qkv[:, t, o:o + w], ps[:, 2 * t + part, 0:w], bqkv[:, o:o + w],
                                        ALU.add).then_inc(qkv_ok, 1)
            dve.wait_ge(qkv_ok, 2 * T)
            E2 = T * NH * HD
            qk4 = qkv[:, :, 0:NH * HD].rearrange("p t (h d) -> p t h d", h=NH)
            work = lru[:, 4096:8192]
            w1, w2, w3 = (work[:, i * E2:(i + 1) * E2] for i in range(3))
            v1, v2, v3 = (w.rearrange("p (t h d) -> p t h d", t=T, h=NH) for w in (w1, w2, w3))
            link(nc.vector.tensor_tensor(v1, qk4, qk4, ALU.mult))
            link(nc.vector.tensor_reduce(qk_rstd, w1.rearrange("p (g d) -> p g d", d=HD), AX.X, ALU.add))
            link(nc.vector.tensor_scalar(qk_rstd, qk_rstd, 1.0 / HD, EPS, ALU.mult, ALU.add))
            nc.vector.reciprocal(qk_rstd, qk_rstd).then_inc(qk_inv, 1)
            dve.wait_ge(qk_rs, 1)
            for t in range(T):
                r = qk_rstd[:, t * NH:(t + 1) * NH].unsqueeze(2).to_broadcast([P, NH, HD])
                link(nc.vector.tensor_tensor(v1[:, t], qk4[:, t], r, ALU.mult))
                link(nc.vector.tensor_tensor(v1[:, t], v1[:, t], gains[:, :].rearrange("p (h d) -> p h d", h=NH),
                                             ALU.mult))
                cos = cst[:, C_COS + t * HD:C_COS + (t + 1) * HD].unsqueeze(1).to_broadcast([P, NH, HD])
                link(nc.vector.tensor_tensor(v2[:, t], v1[:, t], cos, ALU.mult))
                Q4 = HD // 4
                s5 = v1[:, t].rearrange("p h (a b i) -> p h a b i", a=2, b=2)
                d5 = v3[:, t].rearrange("p h (a b i) -> p h a b i", a=2, b=2)
                for b in range(2):
                    for a in range(2):
                        o = C_SIN + t * HD + (2 * a + b) * Q4
                        sin = cst[:, o:o + Q4].unsqueeze(1).to_broadcast([P, NH, Q4])
                        nc.vector.tensor_tensor(d5[:, :, a, b, :], s5[:, :, a, 1 - b, :], sin,
                                                ALU.mult).then_inc(v_step, 1)
                        steps[0] += 1
                dve.wait_ge(v_step, steps[0])
                link(nc.vector.tensor_tensor(qk4[:, t], v2[:, t], v3[:, t], ALU.add))
            kd = k_twice.rearrange("p (t g r d) -> p t g r d", t=T, g=NKV, r=2)
            for t in range(T):
                ins = nc.vector.tensor_copy(
                    kd[:, t], qkv[:, t, QW:QW + KVW].rearrange("p (g d) -> p g d", g=NKV).unsqueeze(2)
                    .to_broadcast([P, NKV, 2, HD]))
                ins.then_inc(rot_ok, 1)

            def lru_unit_work(u):
                rows = lambda b: b.rearrange("p (d c n) -> p d c n", d=2, c=4)
                x4 = xc[:, 4 * u:4 * u + 4, :]
                dve.wait_ge(gate_read, 16 * (u + 1))
                for d in range(2):
                    link(nc.vector.scalar_tensor_tensor(out=rows(lruI)[:, d], in0=rows(lruI)[:, d], scalar=1.0, in1=x4,
                                                        op0=ALU.add, op1=ALU.mult))
                dve.wait_ge(lru_t, 8 * (u + 1))
                nc.vector.scalar_tensor_tensor(out=lruE, in0=lruE, scalar=1.0, in1=lruR, op0=ALU.add,
                                               op1=ALU.mult).then_inc(lru_w, 1)
                dve.wait_ge(lru_s, u + 1)
                link(nc.vector.tensor_tensor(lruI, lruI, lruE, ALU.mult))
                for c in range(4):
                    for d in range(2):
                        a, b, h = rows(lruA)[:, d, c, :], rows(lruI)[:, d, c, :], rows(lruR)[:, d, c, :]
                        if d == 1:
                            a, b, h = a[:, ::-1], b[:, ::-1], h[:, ::-1]
                        nc.vector.tensor_tensor_scan(h, a, b, 0.0, ALU.mult, ALU.add).then_inc(v_step, 1)
                        steps[0] += 1
                dve.wait_ge(v_step, steps[0])
                nc.vector.tensor_tensor(x4, rows(lruR)[:, 0], rows(lruR)[:, 1], ALU.add).then_inc(lru_unit, 1)

            lru_unit_work(0)
            dve.wait_ge(qk_tp, 3)
            nc.vector.tensor_tensor(wrg, cst[:, C_WR:C_WR + KD * NE].rearrange("p (k e) -> p k e", k=KD),
                                    cst[:, C_G2:C_G2 + KD].unsqueeze(2).to_broadcast([P, KD, NE]),
                                    ALU.mult).then_inc(wrg_ok, 1)
            lru_unit_work(1)
            dve.wait_ge(lru_unit, 2)
            dve.wait_ge(gelu_ok, 1)
            nc.vector.tensor_tensor(xc, xc, gelu[:, :, :], ALU.mult).then_inc(lru_unit, 1)

            def head_max(h):
                b = (h % 2) * T
                dve.wait_ge(score_ps, h + 1)
                link(nc.vector.tensor_reduce(neg_max[:, b:b + T], ps[:, h % 2, :].rearrange("p (t n) -> p t n", t=T),
                                             AX.X, ALU.max))
                nc.vector.tensor_scalar(neg_max[:, b:b + T], neg_max[:, b:b + T], -(HD ** -0.5), None,
                                        ALU.mult).then_inc(max_ok, 1)

            def head_norm(h):
                b = (h % 2) * T
                dve.wait_ge(exp_ok, T * (h + 1))
                link(nc.vector.reciprocal(exp_sum[:, b:b + T], exp_sum[:, b:b + T]))
                for t in range(T):
                    nc.vector.tensor_scalar(prob[:, h % 2, t, :], prob[:, h % 2, t, :], exp_sum[:, b + t:b + t + 1],
                                            None, ALU.mult).then_inc(prob_ok, 1)

            def pair_attn(j):
                dve.wait_ge(pv_ps, 2 * j + 2)
                nc.vector.tensor_copy(attnT[:, j, :], half(3, 0)).then_inc(attn_ok, 1)

            for s in range(NQ + 3):
                if s < NQ:
                    head_max(s)
                    head_norm(s)
                if s >= 3 and (s - 3) % 2 == 1:
                    pair_attn((s - 3) // 2)

            for g in range(KD):
                o = (g % 2) * TOK
                dve.wait_ge(branch_ps, g + 1)
                nc.vector.scalar_tensor_tensor(out=m_a[:, o:o + TOK], in0=gA[:, g, :], scalar=1.0,
                                               in1=half(4 + g % 2, 0), op0=ALU.add, op1=ALU.mult)
                link(nc.vector.scalar_tensor_tensor(out=m_r[:, o:o + TOK], in0=gR[:, g, :], scalar=1.0,
                                                    in1=half(4 + g % 2, 1), op0=ALU.add, op1=ALU.mult))
                nc.vector.tensor_tensor(mergedT[:, g, :], m_a[:, o:o + TOK], m_r[:, o:o + TOK],
                                        ALU.add).then_inc(merged_ok, 1)
            dve.wait_ge(mixed_ps, 2)
            for n in range(2 * T):
                t, o = n // 2, (n % 2) * BANK
                nc.vector.scalar_tensor_tensor(out=x_sb[:, t, o:o + BANK], in0=ps[:, n, :], scalar=0.5,
                                               in1=x_sb[:, t, o:o + BANK], op0=ALU.mult, op1=ALU.add).then_inc(x2_ok, 1)
            for b in range(2):
                dve.wait_ge(tposed, 8 + 2 * b + 2)
                nc.vector.tensor_copy(x2T[:, 2 * b:2 * b + 2, :].rearrange("p k n -> p (k n)"),
                                      ps[:, 4 + b, :]).then_inc(xT_v, 1)
            inverse_variance(1, sq_sum, D, 2 * T)

            link(nc.vector.memset(rank_col[:, :, :], -1.0))
            dve.wait_ge(late_in, 48)
            dve.wait_ge(rstd_ok, 2)
            dve.wait_ge(logit_ps, 1)
            for t in range(T):
                link(nc.vector.scalar_tensor_tensor(out=logit[:, t, :], in0=ps[:, 4, t * NE:(t + 1) * NE],
                                                    scalar=rstd[:, t:t + 1], in1=brt[:, :], op0=ALU.mult, op1=ALU.add))
            for t in range(T):
                link(nc.vector.max(top8[:, t, :], logit[:, t, :]))
                link(nc.vector.max_index(idx_u[:, t, :], top8[:, t, :], logit[:, t, :]))
            nc.vector.tensor_scalar(nmax.unsqueeze(2), top8[:, :, 0:1], -1.0, None, ALU.mult).then_inc(top_ok, 1)
            link(nc.vector.tensor_copy(idx_f, idx_u[:, :, :]))
            expert_no = slotno[:, 0:NE].unsqueeze(1).to_broadcast([P, TOPK, NE])
            for t in range(T):
                link(nc.vector.tensor_tensor(hot[:, t], expert_no,
                                             idx_f[:, t, 0:TOPK].unsqueeze(2).to_broadcast([P, TOPK, NE]),
                                             ALU.is_equal))
                nc.vector.tensor_reduce(mask[:, t, :], hot[:, t].rearrange("p k e -> p e k"), AX.X,
                                        ALU.add).then_inc(mask_ok, 1)
            dve.wait_ge(ex_ok, T)
            link(nc.vector.reciprocal(einv, esum))
            for t in range(T):
                link(nc.vector.tensor_scalar(g4[:, t, :], ex4[:, t, :], einv[:, t:t + 1], None, ALU.mult))
                link(nc.vector.tensor_tensor(hotg[:, t], hot[:, t],
                                             g4[:, t, :].unsqueeze(2).to_broadcast([P, TOPK, NE]), ALU.mult))
                nc.vector.tensor_reduce(gate[:, t, :], hotg[:, t].rearrange("p k e -> p e k"), AX.X,
                                        ALU.add).then_inc(mask_ok, 1)
            dve.wait_ge(gateT_ps, 1)
            nc.vector.tensor_copy(gateT, ps[0:NE, 6, 0:TOK]).then_inc(gateT_ok, 1)
            dve.wait_ge(rank_ps, 1)
            link(nc.vector.tensor_reduce(cmax, ps[0:1, 5, 2 * NE:3 * NE], AX.X, ALU.max))
            link(nc.vector.tensor_scalar(rnd, cmax, float(CAP), 1.0, ALU.is_gt, ALU.add))
            for r in range(2, ROUNDS):
                link(nc.vector.tensor_scalar(rnd2, cmax, float(CAP * r), None, ALU.is_gt))
                link(nc.vector.tensor_tensor(rnd, rnd, rnd2, ALU.add))
            nc.vector.tensor_scalar(passes[:, :], rnd, float(NE), None, ALU.mult).then_inc(passes_ok, 1)
            link(nc.vector.scalar_tensor_tensor(out=ranked.rearrange("p t e -> p (t e)"), in0=ps[:, 5, 0:T * NE],
                                                scalar=FAR, in1=mask.rearrange("p t e -> p (t e)"),
                                                op0=ALU.add, op1=ALU.mult))
            dve.wait_ge(mask_ok, 2 * T)
            for r in range(ROUNDS):
                nc.vector.tensor_scalar(rank_col[:, :, r * NE:(r + 1) * NE], ranked, -FAR - CAP * r, None,
                                        ALU.add).then_inc(cols_ok, 1)
                nc.vector.tensor_copy(gate_col[:, :, r * NE:(r + 1) * NE], gate).then_inc(cols_ok, 1)

            dve.wait_ge(cols_ok, 2 * ROUNDS)
            for t in range(T):
                nc.vector.tensor_scalar(sel_next[:, t, :], slotno[:, 0:CAP], rank_col[:, t, 0:1], None,
                                        ALU.is_equal).then_inc(sel_ok, 1)
            gain2 = cst[:, C_G2:C_G2 + KD].unsqueeze(2).to_broadcast([P, KD, CAP])
            nc.vector.memset(sgT[1], 0.0).then_inc(sg_ok, 2)
            nc.vector.memset(pair_out[1], 0.0).then_inc(out_ok, 1)
            dve.wait_ge(xg_ps, 1)
            nc.vector.tensor_tensor(xgT, ps[:, 7, :].rearrange("p (k n) -> p k n", k=KD), gain2,
                                    ALU.mult).then_inc(xg_ok, 1)
            gv = gub.rearrange("p (j h n) -> p j h n", j=KD, h=2)
            as3 = lambda b: b.rearrange("p (j n) -> p j n", j=KD)
            n_pass = dve.value_load(passes[0:1, 0:1], min_val=NE, max_val=NE * ROUNDS)
            with dve.Fori(0, n_pass, UNROLL) as n:
                for i in range(UNROLL):
                    n0 = dve.snap(n + i)
                    n1 = dve.snap(n + i + 1)
                    n2 = dve.snap(n + i + 2)
                    e16 = dve.snap(((n + i) & (NE - 1)) * 16)
                    dve.wait_ge(chunk_used[3], n1)
                    nc.vector.tensor_copy(gu_sb[:, 0:BANK], ps[:, 4, :]).then_inc(gu_v, 1)
                    for t in range(T):
                        nc.vector.tensor_scalar(sel_next[:, t, :], slotno[:, 0:CAP], rank_col[:, t, bass.ds(n1, 1)],
                                                None, ALU.is_equal).then_inc(sel_ok, 1)
                    for t in range(T):
                        o = i % 2 * CAP
                        nc.vector.tensor_scalar(sel_gate[:, t, o:o + CAP], slotno[:, 0:CAP],
                                                rank_col[:, t, bass.ds(n0, 1)], gate_col[:, t, bass.ds(n0, 1)],
                                                ALU.is_equal, ALU.mult).then_inc(sgate_ok, 1)
                    dve.wait_ge(tp_ps, n1)
                    nc.vector.tensor_tensor(gub.rearrange("p (j n) -> p j n", j=16),
                                            ps[:, 6:8, :].rearrange("p b (j n) -> p (b j) n", n=CAP),
                                            cst[:, bass.ds(e16 + C_BGU, 16)].unsqueeze(2).to_broadcast([P, 16, CAP]),
                                            ALU.add).then_inc(tp_read, 1)
                    dve.wait_ge(tp_read, n1)
                    nc.vector.tensor_scalar(as3(g_cl), gv[:, :, 0, :], LIMIT, None, ALU.min).then_inc(g_ok, 1)
                    nc.vector.tensor_scalar(as3(u_cl), gv[:, :, 1, :], LIMIT, -LIMIT, ALU.min, ALU.max).then_inc(u_ok, 1)
                    dve.wait_ge(g_ok, n1)
                    dve.wait_ge(u_ok, n1)
                    nc.vector.scalar_tensor_tensor(out=act1, in0=u_cl, scalar=1.0, in1=g_cl, op0=ALU.add,
                                                   op1=ALU.mult).then_inc(a1_ok, 1)
                    dve.wait_ge(a1_ok, n1)
                    dve.wait_ge(sig_ok, n1)
                    nc.vector.tensor_tensor(actT, as3(act1), as3(sig), ALU.mult).then_inc(act_ok, 1)
                    dve.wait_ge(xg_ps, n2)
                    nc.vector.tensor_tensor(xgT, ps[:, 7, :].rearrange("p (k n) -> p k n", k=KD), gain2,
                                            ALU.mult).then_inc(xg_ok, 1)
                    if i % 2 == 1:
                        dve.wait_ge(sg_ps, n1)
                        nc.vector.tensor_copy(sgT[i // 2], ps[:, 4, 0:T * P].rearrange("p (t n) -> p t n", t=T)
                                              ).then_inc(sg_ok, 2)

            for n in range(2 * T):
                t, o = n // 2, (n % 2) * BANK
                dve.wait_ge(y_ok, n + 1)
                nc.vector.tensor_tensor(x_sb[:, t, o:o + BANK], ps[:, n, :], x_sb[:, t, o:o + BANK],
                                        ALU.add).then_inc(x3_ok, 1)
            inverse_variance(2, sq_sum, D, 3 * T)
            dve.wait_ge(rstd_ok, 3)
            for t in range(T):
                nc.vector.scalar_tensor_tensor(out=x_sb[:, t, :], in0=x_sb[:, t, :], scalar=rstd[:, t:t + 1],
                                               in1=fin_g, op0=ALU.mult, op1=ALU.mult).then_inc(fin_ok, 1)

        @block.tensor
        def _(pe):
            def chunk_in(c):
                pe.wait_ge(slot_full[slot_of(c)], 16 * (use_of(c) + 1))

            def transposes(rows, tp0):
                for k in range(KD):
                    for t in range(T):
                        o = (k % 2) * TOK + t * P
                        ins = nc.tensor.transpose(ps[:, tp0 + k // 2, o:o + P], rows[:, t, k::KD], ident)
                    ins.then_inc(tposed, 1)

            def group(i):
                c = i // 4 if i < 8 else i // 4 + 3
                w = ring[:, slot_of(c), :].rearrange("p (k n) -> p k n", k=KD)
                if i % 4 == 0:
                    chunk_in(c)
                if i >= 4:
                    pe.wait_ge(group_read, i // 2 * 2 - 2)
                for k in range(KD):
                    ins = nc.tensor.matmul(half(4 + (i // 2) % 2, i % 2), w[:, k, (i % 4) * P:(i % 4 + 1) * P],
                                           hT[:, k, :], start=(k == 0), stop=(k == KD - 1))
                ins.then_inc(group_done, 1)

            def lru_gate_products(u):
                w = ring[:, slot_of(4), :].rearrange("p (m c n) -> p m c n", m=4, c=KD)
                chunk_in(4)
                for c in range(4 * u, 4 * u + 4):
                    pe.wait_ge(conv_ok, c + 1)
                    for m in range(4):
                        n = 4 * c + m
                        if n >= 4:
                            pe.wait_ge(gate_read, n // 2 * 2 - 2)
                        nc.tensor.matmul(half(6 + (n % 4) // 2, n % 2), w[:, m, c, :], xc[:, c, :],
                                         start=True, stop=True).then_inc(gate_ps, 1)

            pe.wait_ge(sq_in, 16)
            pe.wait_ge(normed, T)
            transposes(hn, 0)
            pe.wait_ge(hT_v, 2)
            pe.wait_ge(hT_a, 4)
            for i in range(8):
                group(i)
            for part in range(2):
                chunk_in(2 + part)
                n_col = QW if part == 0 else 2 * KVW
                w = ring[:, slot_of(2 + part), 0:KD * n_col].rearrange("p (k n) -> p k n", k=KD)
                for t in range(T):
                    for k in range(KD):
                        ins = nc.tensor.matmul(ps[:, 2 * t + part, 0:n_col], hT[:, k, t * P:(t + 1) * P], w[:, k, :],
                                               start=(k == 0), stop=(k == KD - 1))
                    ins.then_inc(qkv_done, 1)
            lru_gate_products(0)
            for i in range(8, 12):
                group(i)
            pe.wait_ge(rot_ok, T)
            kd = k_twice.rearrange("p (t g n) -> p t g n", t=T, g=NKV)
            for j in range(2):
                for jj in range(2):
                    for t in range(T):
                        a = 2 * j + jj
                        ins = nc.tensor.transpose(ps[:, j, jj * TOK + t * P:jj * TOK + (t + 1) * P],
                                                  qkv[:, t, a * P:(a + 1) * P], ident)
                ins.then_inc(qk_tp, 1)
            for g in range(NKV):
                for t in range(T):
                    ins = nc.tensor.transpose(ps[:, 2, g * TOK + t * P:g * TOK + (t + 1) * P], kd[:, t, g, :], ident)
            ins.then_inc(qk_tp, 1)
            for i in range(12, 16):
                group(i)
            lru_gate_products(1)

            def scores(h):
                rs = slice(64 * (h % 2), 64 * (h % 2) + 64)
                if h >= 2:
                    pe.wait_ge(exp_ok, T * (h - 1))
                for t in range(T):
                    ins = nc.tensor.matmul(ps[:, h % 2, t * TOK:(t + 1) * TOK], qT[rs, h // 2, t * P:(t + 1) * P],
                                           kT[rs, h // (NQ // NKV), :], start=True, stop=True)
                ins.then_inc(score_ps, 1)

            def prob_transposes(h):
                pe.wait_ge(prob_ok, T * (h + 1))
                if h >= 1:
                    pe.wait_ge(pT_ok, h)
                for kt in range(T):
                    for t in range(T):
                        ins = nc.tensor.transpose(ps[:, 2, kt * TOK + t * P:kt * TOK + (t + 1) * P],
                                                  prob[:, h % 2, t, kt * P:(kt + 1) * P], ident)
                ins.then_inc(pT_ps, 1)

            def values(h):
                g = h // (NQ // NKV)
                o = QW + KVW + g * HD
                pe.wait_ge(pT_ok, h + 1)
                if h >= 2:
                    pe.wait_ge(attn_ok, h // 2)
                for kt in range(T):
                    ins = nc.tensor.matmul(ps[64 * (h % 2):64 * (h % 2) + 64, 3, 0:TOK],
                                           qkv[:, kt, o:o + HD], probT[:, h % 2, kt, :],
                                           start=(kt == 0), stop=(kt == T - 1))
                ins.then_inc(pv_ps, 1)

            for i in range(16, 32):
                group(i)
                s = i - 21
                if s == 0:
                    pe.wait_ge(qk_cp, 3)
                if 0 <= s - 2 < NQ:
                    prob_transposes(s - 2)
                if 0 <= s < NQ:
                    scores(s)
                if 0 <= s - 3 < NQ:
                    values(s - 3)

            wA = ring[:, slot_of(11), :].rearrange("p (k n) -> p k n", k=4)
            wR = [ring[:, slot_of(12 + i), :].rearrange("p (k n) -> p k n", k=4) for i in range(2)]
            wO = [ring[:, slot_of(14 + i), :].rearrange("p (k n) -> p k n", k=4) for i in range(2)]

            def mix(c):
                if c % 4 == 0:
                    chunk_in(14 + c // 4)
                pe.wait_ge(merged_ok, c + 1)
                for n in range(2 * T):
                    t, o = n // 2, (n % 2) * BANK
                    ins = nc.tensor.matmul(ps[:, n, :], mergedT[:, c, t * P:(t + 1) * P], wO[c // 4][:, c % 4, o:o + BANK],
                                           start=(c == 0), stop=(c == KD - 1))
                if c % 4 == 3:
                    ins.then_inc(mixed_ps, 1)

            for g in range(KD):
                cols = slice(g * P, (g + 1) * P)
                if g == 0:
                    for c in range(11, 14):
                        chunk_in(c)
                    pe.wait_ge(lru_unit, 3)
                    pe.wait_ge(attn_ok, 4)
                    pe.wait_ge(group_read, 32)
                if g >= 2:
                    pe.wait_ge(merged_ok, g - 1)
                for k in range(KD):
                    nc.tensor.matmul(half(4 + g % 2, 1), wR[k // 4][:, k % 4, cols], xc[:, k, :],
                                     start=(k == 0), stop=(k == KD - 1))
                for k in range(4):
                    ins = nc.tensor.matmul(half(4 + g % 2, 0), wA[:, k, cols], attnT[:, k, :],
                                           start=(k == 0), stop=(k == 3))
                ins.then_inc(branch_ps, 1)
                if g >= 1:
                    mix(g - 1)
            mix(KD - 1)

            pe.wait_ge(x2_ok, 2 * T)
            transposes(x_sb, 4)
            pe.wait_ge(xT_v, 2)
            pe.wait_ge(xT_a, 2)
            pe.wait_ge(wrg_ok, 1)
            for t in range(T):
                for k in range(KD):
                    ins = nc.tensor.matmul(ps[:, 4, t * NE:(t + 1) * NE], x2T[:, k, t * P:(t + 1) * P], wrg[:, k, :],
                                           start=(k == 0), stop=(k == KD - 1))
            ins.then_inc(logit_ps, 1)
            pe.wait_ge(mask_ok, T)
            nc.tensor.matmul(ps[:, 5, 0:NE], upper, mask[:, 0, :], start=True, stop=True)
            nc.tensor.matmul(ps[:, 5, NE:2 * NE], ones, mask[:, 0, :], start=True, stop=False)
            nc.tensor.matmul(ps[:, 5, NE:2 * NE], upper, mask[:, 1, :], start=False, stop=True)
            for t in range(T):
                ins = nc.tensor.matmul(ps[:, 5, 2 * NE:3 * NE], ones, mask[:, t, :], start=(t == 0), stop=(t == T - 1))
            ins.then_inc(rank_ps, 1)
            pe.wait_ge(mask_ok, 2 * T)
            for t in range(T):
                ins = nc.tensor.transpose(ps[0:NE, 6, t * P:(t + 1) * P], gate[:, t, :], ident)
            ins.then_inc(gateT_ps, 1)

            def gather():
                for k in range(KD):
                    for t in range(T):
                        ins = nc.tensor.matmul(ps[:, 7, k * CAP:(k + 1) * CAP], hn[:, t, k::KD], sel_next[:, t, :],
                                               start=(t == 0), stop=(t == T - 1))
                return ins

            pe.wait_ge(gateT_ok, 1)
            pe.wait_ge(late_in, 48)
            for n in range(2 * T):
                t, o = n // 2, (n % 2) * BANK
                ins = nc.tensor.matmul(ps[:, n, :], gateT[:, t * P:(t + 1) * P], bdn[:, o:o + BANK],
                                       start=True, stop=False)
            ins.then_inc(ybias, 1)
            pe.wait_ge(sel_ok, T)
            pe.wait_ge(normed, 2 * T)
            gather().then_inc(xg_ps, 1)
            pe.wait_ge(ybias, 1)

            def scatter(pair, n, last=False):
                return nc.tensor.matmul(ps[:, n, :], sgT[pair][:, n // 2, :],
                                        pair_out[pair][:, (n % 2) * BANK:(n % 2 + 1) * BANK], start=False, stop=last)

            n_pass = pe.value_load(passes[0:1, 0:1], min_val=NE, max_val=NE * ROUNDS)
            with pe.Fori(0, n_pass, UNROLL) as n:
                for i in range(UNROLL):
                    n1 = pe.snap(n + i + 1)
                    n2 = pe.snap(n + i + 2)
                    sel_n = pe.snap((n + i) * T + 2 * T)
                    use = [EARLIER[SLOT_ORDER[(PER * i + j) % SLOTS]] + (PER * i + j) // SLOTS + 1 for j in range(PER)]
                    full = {u: pe.snap(n * (16 * PER // SLOTS) + 16 * u) for u in sorted(set(use))}
                    if i % 2 == 0:
                        out_n = pe.snap((n + i) * 2 + 1)
                    else:
                        sgate_n = pe.snap((n + i) * T + T)
                    last_pair = (i // 2 + 1) % 2
                    pe.wait_ge(xg_ok, n1)
                    if i % 2 == 0:
                        pe.wait_ge(sg_ok, n2)
                    for j in range(4):
                        s = SLOT_ORDER[(PER * i + j) % SLOTS]
                        pe.wait_ge(slot_full[s], full[use[j]])
                        w = slot(s).rearrange("p (r n) -> p r n", r=2)
                        for r in range(2):
                            k = 2 * j + r
                            for b in range(2):
                                for side in range(2):
                                    o = side * FF + b * BANK
                                    ins = nc.tensor.matmul(ps[64 * side:64 * side + 64, 4 + b, :], xgT[:, k, :],
                                                           w[:, r, o:o + BANK], start=(k == 0), stop=(k == KD - 1))
                        ins.then_inc(chunk_used[j], 1)
                    if i % 2 == 0:
                        pe.wait_ge(out_ok, out_n)
                    scatter(last_pair, 2 * (i % 2))
                    pe.wait_ge(gu_v, n1)
                    pe.wait_ge(gu_a, n1)
                    for j in range(KD):
                        o = (j % 4) * P
                        ins = nc.tensor.transpose(ps[:, 6 + j // 4, o:o + P], gu_sb[:, j::KD], ident)
                    ins.then_inc(tp_ps, 1)
                    scatter(last_pair, 2 * (i % 2) + 1)
                    pe.wait_ge(sel_ok, sel_n)
                    pe.wait_ge(tp_read, n1)
                    gather().then_inc(xg_ps, 1)
                    if i % 2 == 1:
                        pe.wait_ge(sgate_ok, sgate_n)
                        for t in range(T):
                            ins = nc.tensor.transpose(ps[:, 4, t * P:(t + 1) * P], sel_gate[:, t, :], ident)
                        ins.then_inc(sg_ps, 2)
                    pe.wait_ge(act_ok, n1)
                    for j in range(4, PER):
                        s = SLOT_ORDER[(PER * i + j) % SLOTS]
                        pe.wait_ge(slot_full[s], full[use[j]])
                        w = slot(s).rearrange("p (r n) -> p r n", r=4)
                        for r in range(4):
                            k = 4 * (j - 4) + r
                            for side in range(2):
                                ins = nc.tensor.matmul(ps[64 * side:64 * side + 64, 6, :], actT[:, k, :],
                                                       w[:, r, side * BANK:(side + 1) * BANK],
                                                       start=(k == 0), stop=(k == KD - 1))
                        ins.then_inc(chunk_used[j], 1)
            last = pe.snap(n_pass * 2 + 1)
            last_sg = pe.snap(n_pass + 2)
            pe.wait_ge(out_ok, last)
            pe.wait_ge(sg_ok, last_sg)
            for n in range(2 * T):
                scatter(1, n, True).then_inc(y_ok, 1)


def _layouts(a):
    w_in = a["w_in"][0].reshape(P, KD, -1)
    o = QKV
    parts = [w_in[:, :, o:o + 512], w_in[:, :, o + 512:o + 1024], w_in[:, :, 0:QW]]
    gates = np.zeros((P, 4, KD, P), np.float32)
    for m, w in enumerate((a["lru_wa"][0, 0], a["lru_wi"][0, 0], a["lru_wa"][0, 1], a["lru_wi"][0, 1])):
        for r in range(2):
            rs = slice(64 * r, 64 * r + 64)
            gates[rs, m, :, rs] = w[r::2].transpose(1, 0, 2)
    kv = w_in[:, :, QW:QKV].reshape(P, -1)
    kv = np.concatenate([kv, np.zeros((P, CH - kv.shape[1]), np.float32)], axis=1)
    rest = [w_in[:, :, o + 1024 + 512 * i:o + 1536 + 512 * i] for i in range(6)]
    rows4 = lambda w: [w.reshape(-1, 4, P, D)[i].transpose(1, 0, 2) for i in range(w.shape[0] // 512)]
    chunks = parts + [kv, gates] + rest + rows4(a["w_attn_o"][0]) + rows4(a["w_lru_o"][0]) + rows4(a["w_out"][0])
    pre = np.stack([np.ascontiguousarray(c).reshape(P, CH) for c in chunks])

    chan = lambda v: v.reshape(-1, P).T
    rows = TOK // GRID_W
    f32 = np.float32
    inv = THETA ** (-np.arange(0, HD // 2, 2, dtype=f32) / (HD // 2))
    row = np.repeat(np.arange(rows), GRID_W).astype(f32)
    colm = np.tile(np.arange(GRID_W), rows).astype(f32)
    ang_r, ang_c = row[:, None] * inv[None], colm[:, None] * inv[None]
    cos = np.concatenate([np.cos(ang_r)] * 2 + [np.cos(ang_c)] * 2, axis=1).astype(f32)
    sin = np.concatenate([-np.sin(ang_r), np.sin(ang_r), -np.sin(ang_c), np.sin(ang_c)], axis=1).astype(f32)
    tiles = lambda t: t.reshape(T, P, HD).transpose(1, 0, 2).reshape(P, -1)
    lb = np.concatenate([chan(a[k][0, d]) for d in range(2) for k in ("lru_ba", "lru_bi")], axis=1)
    bgu = a["b_gu"][0].reshape(NE, 2, P, KD).transpose(2, 0, 3, 1).reshape(P, -1)
    wr = a["w_router"][0].reshape(P, KD * NE)
    consts = np.concatenate([
        a["norm1_g"][0].reshape(P, KD), a["norm2_g"][0].reshape(P, KD), chan(a["b_in"][0][QKV:]),
        *[chan(a["conv_w"][0, j]) for j in range(TAPS)], chan(a["conv_b"][0]), lb,
        chan(a["lru_lambda"][0, 0]), chan(a["lru_lambda"][0, 1]), tiles(cos), tiles(sin), bgu, wr], axis=1)
    squares = np.stack([np.eye(P), np.triu(np.ones((P, P)), 1), np.ones((P, P)),
                        np.tile(np.arange(CAP), (P, P // CAP))], axis=1).astype(f32)
    one_row = np.concatenate([a["b_in"][0][:QKV], a["q_norm_g"][0], a["k_norm_g"][0], a["b_router"][0],
                              a["final_g"]])[None]
    return {"x": a["x"].reshape(TOK, D), "consts": consts, "squares": squares, "rows": one_row, "pre": pre,
            "w_gu": a["w_gu"][0], "w_down": a["w_down"][0], "b_down": a["b_down"][0]}


def kernel(**inputs):
    import concourse.bacc as _bacc
    from concourse.bass_utils import run_bass_kernel_spmd as _run

    arrays = _layouts({k: np.asarray(v) for k, v in inputs.items()})
    nc = _bacc.Bacc("TRN2", target_bir_lowering=False, num_devices=1, dynamic_dma_scratch_size=1024)
    feed, args = {}, []
    for name, a in arrays.items():
        a = np.ascontiguousarray(a)
        feed[f"in_{name}_dram"] = a
        args.append(nc.dram_tensor(f"in_{name}_dram", a.shape, mybir.dt.from_np(a.dtype), kind="ExternalInput").ap())
    args.append(nc.dram_tensor("out_0_dram", (TOK, D), mybir.dt.float32, kind="ExternalOutput").ap())
    encoder_layer(nc, *args)
    r = _run(nc, [feed], core_ids=[0])
    return r.results[0]["out_0_dram"].reshape(1, TOK, D)
```

```python
import numpy as np
import concourse.bass as bass
from concourse import mybir
from contextlib import ExitStack

P = 128
D = 1024
TOK = 256
T = TOK // P
KD = D // P
HD = 64
NQ, NKV = 8, 2
NH = NQ + NKV
QW, KVW = NQ * HD, NKV * HD
QKV = QW + 2 * KVW
GRID_W = 64
THETA = 10000.0
EPS = 1e-6
RG_C = 8.0
TAPS, PAD_L, PAD_R = 4, 1, 2
NE, TOPK = 32, 4
FF = 1024
LIMIT, ALPHA = 7.0, 1.702
BANK = 512
CH = 4096
SLOTS = 8
PAIRS = 3
PRE = 15
PER = 6
UNROLL = 4
CAP = 64
ROUNDS = TOK // CAP
FAR = 4096.0

C_G1, C_G2, C_BIN, C_CW, C_CB, C_LB, C_LAM, C_COS, C_SIN, C_BGU, C_WR = (
    0, 8, 16, 48, 80, 88, 120, 136, 264, 392, 904)
C_ALL = C_WR + KD * NE


def encoder_layer(nc, x, consts, squares, rows, pre, w_lru, w_gu, w_down, b_down, out):
    f32, f32r, bf16, i32, u32 = (mybir.dt.float32, mybir.dt.float32r, mybir.dt.bfloat16, mybir.dt.int32,
                                 mybir.dt.uint32)
    ALU, ACT, AX = mybir.AluOpType, mybir.ActivationFunctionType, mybir.AxisListType

    ctx = ExitStack()
    with ctx:
        def sb(name, shape, dt=f32):
            return ctx.enter_context(nc.sbuf_tensor(name, shape, dt))

        def sem(name):
            return ctx.enter_context(nc.semaphore(name))

        twice = ([(f"slot{i}", [P, CH]) for i in range(SLOTS - 1)]
                 + [("wide", [P, CH]), ("lru", [P, 4 * 2048]), ("qT", [P, NQ // 2, TOK])])
        with ExitStack() as rounded:
            *ring_r, wide_r, lru_r, qT_r = (rounded.enter_context(nc.sbuf_tensor(n + "_r", s, f32r)) for n, s in twice)
        *ring, wide, lru, qT = (sb(n, s) for n, s in twice)
        LOWS = 2 * PAIRS
        kn = lambda b: b.rearrange("p (k n) -> p k n", n=TOK)
        hT = kn(ring[LOWS][:, 0:KD * TOK])
        hT_lo, hT_hi = kn(ring_r[LOWS][:, 0:KD * TOK]), kn(wide_r[:, 0:KD * TOK])
        lru_w_sb = ring[LOWS][:, KD * TOK:].rearrange("p (m c n) -> p m c n", m=4, c=4)
        xc = kn(wide[:, KD * TOK:])
        x_sb = sb("x_sb", [P, T, D])
        hn = sb("hn", [P, T, D])
        MARGIN = PAD_L + TOK + PAD_R
        xr_flat = sb("xr_flat", [P, KD * MARGIN])
        xr = xr_flat[:, :].rearrange("p (k n) -> p k n", k=KD)
        gR = xr_flat[:, 0:KD * TOK].rearrange("p (k n) -> p k n", k=KD)
        gelu = sb("gelu", [P, KD, TOK])
        qkv = sb("qkv", [P, T, QKV])
        attnT = qT
        kT = sb("kT", [P, NKV, TOK])
        pbuf = sb("pbuf", [P, 4 * T * TOK])
        prob = pbuf[:, 0:2 * T * TOK].rearrange("p (a t n) -> p a t n", a=2, t=T)
        probT = pbuf[:, 2 * T * TOK:].rearrange("p (a t n) -> p a t n", a=2, t=T)
        bqkv, gains = pbuf[:, 0:QKV], pbuf[:, QKV:QKV + NH * HD]
        k_twice = pbuf[:, QKV + NH * HD:QKV + NH * HD + T * NKV * P]
        cst = sb("cst", [P, C_ALL])
        sq = sb("sq", [P, 4, P])
        brt = sb("brt", [P, NE])
        small = sb("small", [P, 256])

        ident, upper, ones, slotno = (sq[:, i, :] for i in range(4))
        hb = cst[:, C_BIN + 16:C_BIN + 32]
        gA = hn[:, :, :].rearrange("p t d -> p (t d)").rearrange("p (k n) -> p k n", k=KD)

        col = [0]

        def scratch(n):
            col[0] += n
            return small[:, col[0] - n:col[0]]

        ssum, rstd = scratch(2), scratch(2)
        qk_rstd = scratch(T * NH)
        lam_h, lam_f = scratch(16), scratch(16)
        warm = scratch(1)
        lam_t = [scratch(16) for _ in range(4)]
        neg_max, exp_sum = scratch(4), scratch(4)

        lruR, lruI, lruA, lruE = (lru[:, 2048 * i:2048 * (i + 1)] for i in range(4))
        x2T = lruI.rearrange("p (t k n) -> p t k n", t=T, k=KD)
        rec_hi, rec_lo = kn(lru_r[:, 2048:4096]), kn(wide_r[:, KD * TOK:])
        merged_hi, merged_lo, merged = kn(lru_r[:, 0:2048]), kn(lru_r[:, 4096:6144]), kn(lruA)
        attn_hi, attn_lo = kn(lru_r[:, 6144:7168]), qT_r[:, :, :]
        m_a, m_r = lruE[:, 1024:1536], lruE[:, 1536:2048]
        at = [0]

        def part(n):
            at[0] += n
            return lru[:, at[0] - n:at[0]]

        gu_sb, gub = part(2 * BANK), part(2 * BANK)
        xgT = part(KD * CAP).rearrange("p (k n) -> p k n", k=KD)
        g_cl, sig, act1, u_cl = (part(KD * CAP) for _ in range(4))
        actT = part(KD * CAP).rearrange("p (k n) -> p k n", k=KD)
        pair_out = [part(D) for _ in range(2)]
        sel_next = part(T * CAP).rearrange("p (t n) -> p t n", t=T)
        sel_gate = part(T * P).rearrange("p (t n) -> p t n", t=T)
        sgT = [part(T * P).rearrange("p (t n) -> p t n", t=T) for _ in range(2)]
        NCOL = (ROUNDS + 1) * NE
        pflat, tflat = pbuf[:, 0:1024], pbuf[:, 1024:2048]
        rank_col = pflat[:, 0:T * NCOL].rearrange("p (t n) -> p t n", t=T)
        gate_col = pflat[:, T * NCOL:2 * T * NCOL].rearrange("p (t n) -> p t n", t=T)
        logit = tflat[:, 0:64].rearrange("p (t e) -> p t e", t=T)
        top8 = tflat[:, 64:80].rearrange("p (t k) -> p t k", t=T)
        idx_f = tflat[:, 80:96].rearrange("p (t k) -> p t k", t=T)
        ex4 = tflat[:, 96:104].rearrange("p (t k) -> p t k", t=T)
        g4 = tflat[:, 104:112].rearrange("p (t k) -> p t k", t=T)
        nmax, esum, einv = tflat[:, 112:114], tflat[:, 114:116], tflat[:, 116:118]
        hot = tflat[:, 128:384].rearrange("p (t k e) -> p t k e", t=T, k=TOPK)
        hotg = tflat[:, 384:640].rearrange("p (t k e) -> p t k e", t=T, k=TOPK)
        mask = tflat[:, 640:704].rearrange("p (t e) -> p t e", t=T)
        gate = tflat[:, 704:768].rearrange("p (t e) -> p t e", t=T)
        ranked = tflat[:, 768:832].rearrange("p (t e) -> p t e", t=T)
        wrg = qkv[:, 0, 0:KD * NE].rearrange("p (k e) -> p k e", k=KD)
        cmax, rnd, rnd2 = tflat[0:1, 832:833], tflat[0:1, 833:834], tflat[0:1, 834:835]
        idx_u = sb("idx_u", [P, T, 8], u32)
        passes = sb("passes", [1, 1], i32)
        fin_g = gelu[:, 0:4, :].rearrange("p k n -> p (k n)")
        bdn, gateT = pair_out[1][0:NE, :], sgT[1][0:NE, :, :]

        ps = ctx.enter_context(nc.psum_tensor("ps", [P, 8, BANK], f32))

        def half(bank, h):
            return ps[:, bank, h * TOK:(h + 1) * TOK]

        x_in, cst_in, sq_in, bias_in, late_in, out_done_dma = (
            sem(n) for n in ("x_in", "cst_in", "sq_in", "bias_in", "late_in", "out_stored"))
        slot_full = [sem(f"slot_full{i}") for i in range(SLOTS)]
        lruw_in = sem("lru_weights_in")
        split_hi, split_v, split_g = sem("chunk_high"), sem("chunk_low_v"), sem("chunk_low_g")
        h_hi, h_lo_v, h_lo_g, rec_split, attn_split = (
            sem(n) for n in ("h_high", "h_low_v", "h_low_g", "rec_split", "attn_split"))
        chunk_used = [sem(f"chunk_used{j}") for j in range(SLOTS)]
        v_step, a_step = sem("v_step"), sem("a_step")
        sq_sum, var_inv, rstd_ok, normed = sem("sq_sum"), sem("var_inv"), sem("rstd_ok"), sem("normed")
        tposed, hT_v, hT_a = sem("tposed"), sem("hT_v"), sem("hT_a")
        group_done, group_read = sem("group_done"), sem("group_read")
        qkv_done, qkv_ok = sem("qkv_done"), sem("qkv_ok")
        conv_ok, conv_half = sem("conv_ok"), sem("conv_half")
        margins = sem("margins")
        gate_ps, gate_read, lru_x, lru_t, lru_w, lru_s, lru_unit = (
            sem(n) for n in ("lru_gate_ps", "lru_gate_read", "lru_exp", "lru_t", "lru_w", "lru_s", "lru_unit"))
        gelu_ok, xT_v, xT_a, wrg_ok, warm_ok = (
            sem(n) for n in ("gelu_ok", "x2T_v", "x2T_a", "router_weights_ok", "warm_ok"))
        lam_e, lam_ok, hb_ok = sem("lam_exp"), sem("lam_ok"), sem("half_bias_ok")
        qk_inv, qk_rs, rot_ok, qk_tp, qk_cp = sem("qk_inv"), sem("qk_rs"), sem("rot_ok"), sem("qk_tposed"), sem("qk_copied")
        score_ps, max_ok, exp_ok, prob_ok, pT_ps, pT_ok, pv_ps, attn_ok = (
            sem(n) for n in ("score_ps", "max_ok", "exp_ok", "prob_ok", "probT_ps", "probT_ok", "pv_ps", "attn_ok"))
        branch_ps, merged_ok, mixed_ps, x2_ok = sem("branch_ps"), sem("merged_ok"), sem("mixed"), sem("x2_ok")
        logit_ps, top_ok, ex_ok, mask_ok, rank_ps, gateT_ps, cols_ok, passes_ok = (
            sem(n) for n in ("logit_ps", "top_ok", "top_exp_ok", "mask_ok", "rank_ps", "gateT_ps",
                             "cols_ok", "passes_ok"))
        sel_ok, xg_ps, xg_ok, gu_v, gu_a, tp_ps, tp_read, sgate_ok, sg_ps, sg_ok = (
            sem(n) for n in ("sel_ok", "xg_ps", "xg_ok", "gu_copied_v", "gu_copied_a", "tp_ps", "tp_read",
                             "sel_gate_ok", "sgT_ps", "sgT_ok"))
        g_ok, sig_ok, u_ok, a1_ok, act_ok, out_ok, y_ok = (
            sem(n) for n in ("g_clamped", "sigmoid_ok", "u_clamped", "gated_ok", "act_ok", "out_ok", "y_ok"))
        x3_ok, fin_ok, zeros = sem("x3_ok"), sem("fin_ok"), sem("zeros_ok")
        mix_part = sem("mix_part")

        block = ctx.enter_context(nc.Block())

        gu_chunk = w_gu.rearrange("e (p j r) n -> e j p (r n)", j=4, r=2)
        dn_chunk = w_down.rearrange("e (p j r) n -> e j p (r n)", j=2, r=4)

        SLOT_ORDER = [LOWS, 0, 1, 2, 3, SLOTS - 1, 4, 5]
        EARLIER = [PRE // PAIRS if s < LOWS and s % 2 == 0 else 0 for s in range(SLOTS)]
        FREED = {LOWS: [(group_done, 32), (gate_ps, 32)], 0: [(mixed_ps, 1)], 2: [(branch_ps, KD)],
                 SLOTS - 1: [(branch_ps, KD)], 4: [(mixed_ps, 2)]}

        def slot(s):
            return ring[s][:, :] if s < SLOTS - 1 else wide[:, :]

        CONSUMED = ([(group_done, 4), (group_done, 8), (qkv_done, T), (qkv_done, 2 * T)]
                    + [(group_done, 12 + 4 * i) for i in range(6)]
                    + [(branch_ps, 3), (branch_ps, 6), (mixed_ps, 1), (branch_ps, KD), (mixed_ps, 2)])
        IN_CHUNK, Q_CHUNK, BR_CHUNK, MIX_CHUNK = [0, 1, 4, 5, 6, 7, 8, 9], 2, [10, 11, 13], [12, 14]
        WIDTH = [KD * 2 * KVW if c == Q_CHUNK + 1 else CH for c in range(PRE)]

        def low(c):
            return ring_r[2 * (c % PAIRS)][:, 0:WIDTH[c]]

        def high(c):
            return ring_r[2 * (c % PAIRS) + 1][:, 0:WIDTH[c]]

        def whole(c):
            return ring[2 * (c % PAIRS)][:, 0:WIDTH[c]]

        def expert_src(e, j):
            c = gu_chunk[e, j] if j < 4 else dn_chunk[e, j - 4]
            return c if isinstance(e, int) else c.rearrange("o p n -> (o p) n")

        @block.sync
        def _(sp):
            for t in range(T):
                sp.dma_start(x_sb[:, t, :], x[t * P:(t + 1) * P, :]).then_inc(x_in, 16)
            def expert_load(k):
                s = SLOT_ORDER[k % SLOTS]
                if k >= SLOTS:
                    sp.wait_ge(chunk_used[(k - SLOTS) % PER], (k - SLOTS) // PER + 1)
                else:
                    for freed in FREED.get(s, ()):
                        sp.wait_ge(*freed)
                sp.dma_start(slot(s), expert_src(k // PER, k % PER)).then_inc(slot_full[s], 16)

            for c in range(PRE):
                if c >= PAIRS:
                    sp.wait_ge(*CONSUMED[c - PAIRS])
                sp.dma_start(whole(c), pre[c, :, 0:WIDTH[c]]).then_inc(slot_full[2 * (c % PAIRS)], 16)
                if c == 1:
                    sp.dma_start(pbuf[:, 0:QKV + NH * HD], rows[0:1, 0:QKV + NH * HD].to_broadcast([P, QKV + NH * HD])
                                 ).then_inc(bias_in, 16)
                    o = QKV + NH * HD
                    sp.dma_start(brt[:, :], rows[0:1, o:o + NE].to_broadcast([P, NE])).then_inc(bias_in, 16)
                if c == 0:
                    sp.dma_start(ring[LOWS][:, KD * TOK:], w_lru[0]).then_inc(lruw_in, 16)
                if c == MIX_CHUNK[0]:
                    expert_load(0)
                if c == 6:
                    sp.wait_ge(gate_ps, 16)
                    sp.dma_start(ring[LOWS][:, KD * TOK:], w_lru[1]).then_inc(lruw_in, 16)
            for k in range(1, UNROLL * PER):
                expert_load(k)
            sp.wait_ge(passes_ok, 1)
            n_pass = sp.value_load(passes[0:1, 0:1], min_val=NE, max_val=NE * ROUNDS)
            with sp.Fori(UNROLL, n_pass, UNROLL) as n:
                for i in range(UNROLL):
                    e = sp.snap(sp.to_reg((n + i) & (NE - 1)), min_val=0, max_val=NE - 1)
                    used = {q: sp.snap(n + q) for q in sorted({(PER * i + j - SLOTS) // PER + 1 for j in range(PER)})}
                    for j in range(PER):
                        k = PER * i + j
                        s = SLOT_ORDER[k % SLOTS]
                        sp.wait_ge(chunk_used[(k - SLOTS) % PER], used[(k - SLOTS) // PER + 1])
                        sp.dma_start(slot(s), expert_src(bass.ds(e, 1), j)).then_inc(slot_full[s], 16)
            for t in range(T):
                sp.wait_ge(fin_ok, t + 1)
                sp.dma_start(out[t * P:(t + 1) * P, :], x_sb[:, t, :]).then_inc(out_done_dma, 16)
            sp.wait_ge(out_done_dma, 16 * T)

        @block.scalar
        def _(act):
            act.dma_start(sq[:, :, :], squares).then_inc(sq_in, 16)
            act.dma_start(cst[:, :], consts).then_inc(cst_in, 16)
            def sum_squares(turn, ready, value, tiles=range(T)):
                for t in tiles:
                    act.wait_ge(ready, value(t))
                    dst = hn[:, t, :] if turn < 2 else lruA[:, t * D:(t + 1) * D]
                    nc.scalar.activation(dst, x_sb[:, t, :], ACT.Square,
                                         accum_out=ssum[:, t:t + 1]).then_inc(sq_sum, 1)

            def root(turn):
                act.wait_ge(var_inv, turn + 1)
                nc.scalar.activation(rstd, ssum, ACT.Sqrt).then_inc(rstd_ok, 1)

            def load_sqrt_table(times):
                act.wait_ge(warm_ok, times)
                nc.scalar.activation(warm, warm, ACT.Sqrt).then_inc(warm_ok, 1)

            def scaled_copy(g, dst, tp0):
                for k in range(4, 8):
                    act.wait_ge(tposed, k // 2 * 2 + 2)
                    nc.scalar.activation(dst[:, k, :], half(tp0 + k // 2, k % 2), ACT.Copy,
                                         scale=cst[:, g + k:g + k + 1]).then_inc(hT_a, 1)

            def group(i):
                act.wait_ge(group_done, i + 1 if i < 4 else i // 2 * 2 + 2)
                src = half(4 + i, 0) if i < 4 else half(4 + (i // 2) % 2, i % 2)
                if i < 8:
                    if i == 0:
                        act.wait_ge(margins, 1)
                        act.wait_ge(hb_ok, 2)
                    nc.scalar.activation(xr[:, i, PAD_L:PAD_L + TOK], src, ACT.Identity,
                                         bias=cst[:, C_BIN + i:C_BIN + i + 1]).then_inc(group_read, 1)
                elif i < 16:
                    nc.scalar.activation(gelu[:, i - 8, :], src, ACT.Identity,
                                         bias=cst[:, C_BIN + i:C_BIN + i + 1]).then_inc(group_read, 1)
                else:
                    dst = gA[:, i - 16, :] if i < 24 else gR[:, i - 24, :]
                    if i == 24:
                        act.wait_ge(conv_ok, KD)
                    nc.scalar.activation(dst, src, ACT.Tanh, scale=0.5,
                                         bias=hb[:, i - 16:i - 15]).then_inc(group_read, 1)

            def lru_gates(u, blocks):
                if u == 1 and blocks[0] == 0:
                    act.wait_ge(lru_unit, 1)
                for c in blocks:
                    for m in range(4):
                        n = 16 * u + 4 * c + m
                        act.wait_ge(gate_ps, n // 2 * 2 + 2)
                        dst = (lruR if m % 2 == 0 else lruI)[:, (m // 2 * 4 + c) * TOK:(m // 2 * 4 + c + 1) * TOK]
                        b = C_LB + m * 8 + 4 * u + c
                        nc.scalar.activation(dst, half(6 + (n % 4) // 2, n % 2), ACT.Tanh, scale=0.5,
                                             bias=cst[:, b:b + 1]).then_inc(gate_read, 1)

            def lru_decay(u, part):
                blocks = [((4 * d + c) * TOK, 8 * d + 4 * u + c) for d in range(2) for c in range(4)]
                if part == 0:
                    act.wait_ge(gate_read, 16 * (u + 1))
                    act.wait_ge(lam_ok, 1)
                if part < 2:
                    dst, lam = ((lruA, lam_h), (lruE, lam_f))[part]
                    for o, k in blocks:
                        nc.scalar.activation(dst[:, o:o + TOK], lruR[:, o:o + TOK], ACT.Exp, scale=lam[:, k:k + 1],
                                             bias=lam[:, k:k + 1]).then_inc(lru_x, 1)
                else:
                    act.wait_ge(lru_x, 16 * (u + 1))
                    for o, k in blocks:
                        nc.scalar.activation(lruR[:, o:o + TOK], lruR[:, o:o + TOK], ACT.Tanh, scale=lam_h[:, k:k + 1],
                                             bias=lam_h[:, k:k + 1]).then_inc(lru_t, 1)

            def lru_root(u):
                act.wait_ge(lru_w, u + 1)
                nc.scalar.activation(lruE, lruE, ACT.Sqrt, scale=-0.25).then_inc(lru_s, 1)

            def copy_qk():
                for j in range(2):
                    act.wait_ge(qk_tp, j + 1)
                    nc.scalar.activation(qT[:, 2 * j:2 * j + 2, :].rearrange("p a n -> p (a n)"), ps[:, j, :],
                                         ACT.Copy).then_inc(qk_cp, 1)
                act.wait_ge(qk_tp, 3)
                nc.scalar.activation(kT[:, :, :].rearrange("p a n -> p (a n)"), ps[:, 2, :], ACT.Copy).then_inc(qk_cp, 1)

            load_sqrt_table(1)
            sum_squares(0, x_in, lambda t: 16 * T)
            root(0)
            act.wait_ge(cst_in, 16)
            scaled_copy(C_G1, hT, 0)
            act.wait_ge(lam_e, 1)
            nc.scalar.activation(lam_t[1], lam_t[0], ACT.Exp, scale=-1.0).then_inc(lam_e, 1)
            for i in range(8):
                group(i)
            lru_gates(0, range(4))
            act.wait_ge(qk_inv, 1)
            nc.scalar.activation(qk_rstd, qk_rstd, ACT.Sqrt).then_inc(qk_rs, 1)
            for i in range(8, 14):
                group(i)
                if i % 2 == 1:
                    lru_decay(0, i // 2 - 4)
            copy_qk()
            for i in range(14, 16):
                group(i)
            lru_root(0)
            act.wait_ge(group_read, 16)
            gelu_all = gelu[:, :, :].rearrange("p k n -> p (k n)")
            nc.scalar.activation(gelu_all, gelu_all, ACT.Gelu_apprx_tanh).then_inc(gelu_ok, 1)
            for i in range(16, 32):
                if 17 <= i < 21:
                    lru_gates(1, [i - 17])
                s = i - 18
                if 0 <= s - 2 < NQ:
                    h = s - 2
                    act.wait_ge(pT_ps, h + 1)
                    nc.scalar.activation(probT[:, h % 2, :, :].rearrange("p a n -> p (a n)"), ps[:, 2, :],
                                         ACT.Copy).then_inc(pT_ok, 1)
                if 0 <= s < NQ:
                    act.wait_ge(max_ok, s + 1)
                    for t in range(T):
                        b = (s % 2) * T + t
                        nc.scalar.activation(prob[:, s % 2, t, :], ps[:, s % 2, t * TOK:(t + 1) * TOK], ACT.Exp,
                                             bias=neg_max[:, b:b + 1], scale=HD ** -0.5,
                                             accum_out=exp_sum[:, b:b + 1]).then_inc(exp_ok, 1)
                if i % 2 == 1:
                    group(i - 1)
                    group(i)
                if 20 <= i < 23:
                    lru_decay(1, i - 20)
                if i == 24:
                    lru_root(1)
            load_sqrt_table(2)
            act.wait_ge(lru_unit, 3)
            o = QKV + NH * HD
            act.dma_start(fin_g, rows[0:1, o + NE:o + NE + D].to_broadcast([P, D])).then_inc(late_in, 16)
            act.wait_ge(out_ok, 1)
            act.dma_start(bdn, b_down).then_inc(late_in, 16)
            for t in range(T):
                sum_squares(1, x2_ok, lambda t: 2 * t + 2, [t])
                act.wait_ge(tposed, KD + 2 * t + 2)
                nc.scalar.activation(x2T[:, t, 4:8, :].rearrange("p k n -> p (k n)"), ps[:, 5 + 2 * t, :],
                                     ACT.Copy).then_inc(xT_a, 1)
            root(1)
            act.wait_ge(rstd_ok, 2)
            for t in range(T):
                nc.scalar.activation(hn[:, t, :], x_sb[:, t, :], ACT.Copy, scale=rstd[:, t:t + 1]).then_inc(normed, 1)
            for t in range(T):
                act.wait_ge(top_ok, 1)
                nc.scalar.activation(ex4[:, t, :], top8[:, t, 0:TOPK], ACT.Exp, bias=nmax[:, t:t + 1],
                                     accum_out=esum[:, t:t + 1]).then_inc(ex_ok, 1)

            act.wait_ge(passes_ok, 1)
            n_pass = act.value_load(passes[0:1, 0:1], min_val=NE, max_val=NE * ROUNDS)
            with act.Fori(0, n_pass, UNROLL) as n:
                for i in range(UNROLL):
                    n1 = act.snap(n + i + 1)
                    act.wait_ge(chunk_used[3], n1)
                    nc.scalar.activation(gu_sb[:, BANK:2 * BANK], ps[:, 5, :], ACT.Copy).then_inc(gu_a, 1)
                    act.wait_ge(g_ok, n1)
                    nc.scalar.activation(sig, g_cl, ACT.Sigmoid, scale=ALPHA).then_inc(sig_ok, 1)
                    act.wait_ge(chunk_used[5], n1)
                    rs = slice(64 * (i % 2), 64 * (i % 2) + 64)
                    for side in range(2):
                        nc.scalar.activation(pair_out[i // 2][rs, side * BANK:(side + 1) * BANK],
                                             ps[64 * side:64 * side + 64, 6, :], ACT.Copy).then_inc(out_ok, 1)

            load_sqrt_table(3)
            sum_squares(2, x3_ok, lambda t: 2 * t + 2)
            root(2)

        def low_part(engine, dst, whole, hi):
            return engine.tensor_tensor(dst, whole, hi.bitcast(f32), ALU.subtract)

        @block.gpsimd
        def _(gp):
            for c in range(PRE):
                gp.wait_ge(split_hi, c + 1)
                hf = slice(WIDTH[c] // 2, WIDTH[c])
                low_part(nc.gpsimd, low(c)[:, hf], whole(c)[:, hf], high(c)[:, hf]).then_inc(split_g, 1)
                if c == 0:
                    gp.wait_ge(h_hi, 2)
                    low_part(nc.gpsimd, hT_lo[:, 4:8], hT[:, 4:8], hT_hi[:, 4:8]).then_inc(h_lo_g, 1)

        @block.vector
        def _(dve):
            steps = [0]

            def link(ins):
                steps[0] += 1
                ins.then_inc(v_step, 1)
                dve.wait_ge(v_step, steps[0])

            def inverse_variance(turn, total, n, value):
                dve.wait_ge(total, value)
                link(nc.vector.tensor_scalar(ssum, ssum, 1.0 / n, EPS, ALU.mult, ALU.add))
                nc.vector.reciprocal(ssum, ssum).then_inc(var_inv, 1)

            def norm_apply():
                dve.wait_ge(rstd_ok, 1)
                for t in range(T):
                    nc.vector.tensor_scalar(hn[:, t, :], x_sb[:, t, :], rstd[:, t:t + 1], None,
                                            ALU.mult).then_inc(normed, 1)

            def scaled_copy(g, dst, tp0):
                for b in range(2):
                    dve.wait_ge(tposed, 2 * b + 2)
                    nc.vector.tensor_tensor(
                        dst[:, 2 * b:2 * b + 2, :], ps[:, tp0 + b, :].rearrange("p (k n) -> p k n", k=2),
                        cst[:, g + 2 * b:g + 2 * b + 2].unsqueeze(2).to_broadcast([P, 2, TOK]),
                        ALU.mult).then_inc(hT_v, 1)

            nc.vector.memset(warm, 1.0).then_inc(warm_ok, 1)
            nc.vector.memset(xr[:, :, 0:PAD_L], 0.0)
            nc.vector.memset(xr[:, :, PAD_L + TOK:], 0.0).then_inc(margins, 1)
            dve.wait_ge(cst_in, 16)
            nc.vector.tensor_scalar(hb, hb, 0.5, None, ALU.mult).then_inc(hb_ok, 1)
            nc.vector.tensor_scalar(cst[:, C_LB:C_LB + 32], cst[:, C_LB:C_LB + 32], 0.5, None,
                                    ALU.mult).then_inc(hb_ok, 1)
            inverse_variance(0, sq_sum, D, T)
            def high_part(dst, whole):
                return nc.vector.tensor_copy(dst, whole)

            def split_high(c):
                dve.wait_ge(slot_full[2 * (c % PAIRS)], 16 * (c // PAIRS + 1))
                high_part(high(c), whole(c)).then_inc(split_hi, 1)

            def split_low(c):
                dve.wait_ge(split_hi, c + 1)
                hf = slice(0, WIDTH[c] // 2)
                low_part(nc.vector, low(c)[:, hf], whole(c)[:, hf], high(c)[:, hf]).then_inc(split_v, 1)

            def split(c):
                split_high(c)
                split_low(c)

            norm_apply()
            scaled_copy(C_G1, hT, 0)
            dve.wait_ge(hT_v, 2)
            high_part(hT_hi[:, 0:4], hT[:, 0:4]).then_inc(h_hi, 1)
            dve.wait_ge(hT_a, 4)
            high_part(hT_hi[:, 4:8], hT[:, 4:8]).then_inc(h_hi, 1)
            split_high(0)
            split_low(0)
            dve.wait_ge(h_hi, 2)
            low_part(nc.vector, hT_lo[:, 0:4], hT[:, 0:4], hT_hi[:, 0:4]).then_inc(h_lo_v, 1)

            lam = cst[:, C_LAM:C_LAM + 16]
            link(nc.vector.tensor_scalar(lam_t[0], lam, -1.0, None, ALU.mult))
            nc.vector.tensor_tensor(lam_t[0], lam_t[0], lam, ALU.max).then_inc(lam_e, 1)
            split(1)
            split(Q_CHUNK)
            dve.wait_ge(lam_e, 2)
            link(nc.vector.tensor_scalar(lam_t[2], lam_t[1], 2.0, None, ALU.add))
            link(nc.vector.reciprocal(lam_t[2], lam_t[2]))
            link(nc.vector.tensor_tensor(lam_t[1], lam_t[1], lam_t[2], ALU.mult))
            link(nc.vector.tensor_tensor(lam_t[2], lam_t[1], lam_t[1], ALU.mult))
            link(nc.vector.tensor_scalar(lam_t[3], lam_t[2], 1.0 / 17, 1.0 / 15, ALU.mult, ALU.add))
            for q in (13, 11, 9, 7, 5, 3, 1):
                link(nc.vector.tensor_tensor(lam_t[3], lam_t[3], lam_t[2], ALU.mult))
                link(nc.vector.tensor_scalar(lam_t[3], lam_t[3], 1.0 / q, None, ALU.add))
            link(nc.vector.tensor_tensor(lam_t[3], lam_t[3], lam_t[1], ALU.mult))
            link(nc.vector.tensor_scalar(lam_t[0], lam, 0.0, RG_C, ALU.min, ALU.mult))
            link(nc.vector.tensor_scalar(lam_t[3], lam_t[3], 2 * RG_C, None, ALU.mult))
            link(nc.vector.tensor_tensor(lam_f, lam_t[0], lam_t[3], ALU.subtract))
            nc.vector.tensor_scalar(lam_h, lam_f, 0.5, None, ALU.mult).then_inc(lam_ok, 1)

            for c in range(KD):
                if c == 4:
                    split(Q_CHUNK + 1)
                dve.wait_ge(group_read, c + 1)
                w = [cst[:, C_CW + 8 * j + c:C_CW + 8 * j + c + 1] for j in range(TAPS)]
                b = cst[:, C_CB + c:C_CB + c + 1]
                link(nc.vector.tensor_scalar(xc[:, c, :], xr[:, c, 0:TOK], w[0], b, ALU.mult, ALU.add))
                for j in range(1, TAPS):
                    ins = nc.vector.scalar_tensor_tensor(out=xc[:, c, :], in0=xr[:, c, j:j + TOK], scalar=w[j],
                                                         in1=xc[:, c, :], op0=ALU.mult, op1=ALU.add)
                    if j < TAPS - 1:
                        link(ins)
                    else:
                        ins.then_inc(conv_ok, 1)

            dve.wait_ge(bias_in, 32)
            for n in range(2 * T):
                part, t = n // T, n % T
                if n == T:
                    split(4)
                dve.wait_ge(qkv_done, n + 1)
                w = QW if part == 0 else 2 * KVW
                o = 0 if part == 0 else QW
                nc.vector.tensor_tensor(qkv[:, t, o:o + w], ps[:, 2 * t + part, 0:w], bqkv[:, o:o + w],
                                        ALU.add).then_inc(qkv_ok, 1)
            dve.wait_ge(qkv_ok, 2 * T)
            E2 = T * NH * HD
            qk4 = qkv[:, :, 0:NH * HD].rearrange("p t (h d) -> p t h d", h=NH)
            E1 = NH * HD
            w1 = xr_flat[:, 0:E2]
            v1 = w1.rearrange("p (t h d) -> p t h d", t=T, h=NH)
            v2, v3 = (w.rearrange("p (h d) -> p h d", h=NH) for w in (xr_flat[:, E2:E2 + E1], pbuf[:, 0:E1]))
            dve.wait_ge(conv_ok, KD)
            link(nc.vector.tensor_tensor(v1, qk4, qk4, ALU.mult))
            link(nc.vector.tensor_reduce(qk_rstd, w1.rearrange("p (g d) -> p g d", d=HD), AX.X, ALU.add))
            link(nc.vector.tensor_scalar(qk_rstd, qk_rstd, 1.0 / HD, EPS, ALU.mult, ALU.add))
            nc.vector.reciprocal(qk_rstd, qk_rstd).then_inc(qk_inv, 1)
            split(5)
            dve.wait_ge(qk_rs, 1)
            for t in range(T):
                r = qk_rstd[:, t * NH:(t + 1) * NH].unsqueeze(2).to_broadcast([P, NH, HD])
                link(nc.vector.tensor_tensor(v1[:, t], qk4[:, t], r, ALU.mult))
                link(nc.vector.tensor_tensor(v1[:, t], v1[:, t], gains[:, :].rearrange("p (h d) -> p h d", h=NH),
                                             ALU.mult))
                cos = cst[:, C_COS + t * HD:C_COS + (t + 1) * HD].unsqueeze(1).to_broadcast([P, NH, HD])
                link(nc.vector.tensor_tensor(v2, v1[:, t], cos, ALU.mult))
                Q4 = HD // 4
                s5 = v1[:, t].rearrange("p h (a b i) -> p h a b i", a=2, b=2)
                d5 = v3.rearrange("p h (a b i) -> p h a b i", a=2, b=2)
                for b in range(2):
                    for a in range(2):
                        o = C_SIN + t * HD + (2 * a + b) * Q4
                        sin = cst[:, o:o + Q4].unsqueeze(1).to_broadcast([P, NH, Q4])
                        nc.vector.tensor_tensor(d5[:, :, a, b, :], s5[:, :, a, 1 - b, :], sin,
                                                ALU.mult).then_inc(v_step, 1)
                        steps[0] += 1
                dve.wait_ge(v_step, steps[0])
                link(nc.vector.tensor_tensor(qk4[:, t], v2, v3, ALU.add))
            kd = k_twice.rearrange("p (t g r d) -> p t g r d", t=T, g=NKV, r=2)
            for t in range(T):
                ins = nc.vector.tensor_copy(
                    kd[:, t], qkv[:, t, QW:QW + KVW].rearrange("p (g d) -> p g d", g=NKV).unsqueeze(2)
                    .to_broadcast([P, NKV, 2, HD]))
                ins.then_inc(rot_ok, 1)

            rows = lambda b: b.rearrange("p (d c n) -> p d c n", d=2, c=4)

            def lru_input(u):
                dve.wait_ge(gate_read, 16 * (u + 1))
                for d in range(2):
                    link(nc.vector.scalar_tensor_tensor(out=rows(lruI)[:, d], in0=rows(lruI)[:, d], scalar=1.0,
                                                        in1=xc[:, 4 * u:4 * u + 4, :], op0=ALU.add, op1=ALU.mult))

            def lru_square(u):
                dve.wait_ge(lru_t, 8 * (u + 1))
                nc.vector.scalar_tensor_tensor(out=lruE, in0=lruE, scalar=1.0, in1=lruR, op0=ALU.add,
                                               op1=ALU.mult).then_inc(lru_w, 1)

            def lru_scaled(u):
                dve.wait_ge(lru_s, u + 1)
                link(nc.vector.tensor_tensor(lruI, lruI, lruE, ALU.mult))

            def lru_scan(u):
                for c in range(4):
                    for d in range(2):
                        a, b, h = rows(lruA)[:, d, c, :], rows(lruI)[:, d, c, :], rows(lruR)[:, d, c, :]
                        if d == 1:
                            a, b, h = a[:, ::-1], b[:, ::-1], h[:, ::-1]
                        nc.vector.tensor_tensor_scan(h, a, b, 0.0, ALU.mult, ALU.add).then_inc(v_step, 1)
                        steps[0] += 1
                dve.wait_ge(v_step, steps[0])

            def lru_sum(u):
                nc.vector.tensor_tensor(xc[:, 4 * u:4 * u + 4, :], rows(lruR)[:, 0], rows(lruR)[:, 1],
                                        ALU.add).then_inc(lru_unit, 1)

            def recurrent_branch():
                dve.wait_ge(lru_unit, 2)
                dve.wait_ge(gelu_ok, 1)
                nc.vector.tensor_tensor(xc, xc, gelu[:, :, :], ALU.mult).then_inc(lru_unit, 1)

            def recurrent_split():
                dve.wait_ge(lru_unit, 3)
                link(high_part(rec_hi, xc))
                low_part(nc.vector, rec_lo, xc, rec_hi).then_inc(rec_split, 1)

            lru_input(0)
            split(6)
            lru_square(0)
            lru_scaled(0)
            lru_scan(0)
            lru_sum(0)
            dve.wait_ge(qk_tp, 3)
            nc.vector.tensor_tensor(wrg, cst[:, C_WR:C_WR + KD * NE].rearrange("p (k e) -> p k e", k=KD),
                                    cst[:, C_G2:C_G2 + KD].unsqueeze(2).to_broadcast([P, KD, NE]),
                                    ALU.mult).then_inc(wrg_ok, 1)

            def head_max(h):
                b = (h % 2) * T
                dve.wait_ge(score_ps, h + 1)
                link(nc.vector.tensor_reduce(neg_max[:, b:b + T], ps[:, h % 2, :].rearrange("p (t n) -> p t n", t=T),
                                             AX.X, ALU.max))
                nc.vector.tensor_scalar(neg_max[:, b:b + T], neg_max[:, b:b + T], -(HD ** -0.5), None,
                                        ALU.mult).then_inc(max_ok, 1)

            def head_norm(h):
                b = (h % 2) * T
                dve.wait_ge(exp_ok, T * (h + 1))
                link(nc.vector.reciprocal(exp_sum[:, b:b + T], exp_sum[:, b:b + T]))
                for t in range(T):
                    nc.vector.tensor_scalar(prob[:, h % 2, t, :], prob[:, h % 2, t, :], exp_sum[:, b + t:b + t + 1],
                                            None, ALU.mult).then_inc(prob_ok, 1)

            def pair_attn(j):
                dve.wait_ge(pv_ps, 2 * j + 2)
                nc.vector.tensor_copy(attnT[:, j, :], half(3, 0)).then_inc(attn_ok, 1)

            for s in range(NQ + 3):
                if 1 <= s <= NQ:
                    head_norm(s - 1)
                if s < NQ:
                    head_max(s)
                if s >= 4 and s % 2 == 0:
                    pair_attn((s - 4) // 2)
                if s == 0:
                    split(7)
                if s == 1:
                    split(8)
                if s == 3:
                    lru_input(1)
                if s == 4:
                    split(9)
                if s == 5:
                    lru_square(1)
                if s == 7:
                    lru_scaled(1)
                if s == 8:
                    lru_scan(1)
                    split(10)
                if s == 9:
                    lru_sum(1)
                    recurrent_branch()
                if s == 10:
                    recurrent_split()
            dve.wait_ge(attn_ok, NQ // 2)
            link(high_part(attn_hi, attnT[:, :, :]))
            low_part(nc.vector, attn_lo, attnT[:, :, :], attn_hi).then_inc(attn_split, 1)
            split(11)

            for g in range(KD):
                o = (g % 2) * TOK
                dve.wait_ge(branch_ps, g + 1)
                nc.vector.scalar_tensor_tensor(out=m_a[:, o:o + TOK], in0=gA[:, g, :], scalar=1.0,
                                               in1=half(4 + g % 2, 0), op0=ALU.add, op1=ALU.mult)
                link(nc.vector.scalar_tensor_tensor(out=m_r[:, o:o + TOK], in0=gR[:, g, :], scalar=1.0,
                                                    in1=half(4 + g % 2, 1), op0=ALU.add, op1=ALU.mult))
                link(nc.vector.tensor_tensor(merged[:, g, :], m_a[:, o:o + TOK], m_r[:, o:o + TOK], ALU.add))
                link(high_part(merged_hi[:, g, :], merged[:, g, :]))
                low_part(nc.vector, merged_lo[:, g, :], merged[:, g, :], merged_hi[:, g, :]).then_inc(merged_ok, 1)
                if g == 1:
                    split(12)
                if g == 3:
                    split(13)
                if g == 5:
                    split(14)
            dve.wait_ge(merged_ok, KD)
            nc.vector.memset(pair_out[1], 0.0).then_inc(out_ok, 1)
            nc.vector.memset(sgT[1], 0.0).then_inc(zeros, 1)
            nc.vector.memset(sgT[0], 0.0).then_inc(zeros, 1)
            for n in range(2 * T):
                t, o = n // 2, (n % 2) * BANK
                if n < 2 * T - 1:
                    dve.wait_ge(mix_part, n + 1)
                else:
                    dve.wait_ge(mixed_ps, 2)
                nc.vector.scalar_tensor_tensor(out=x_sb[:, t, o:o + BANK], in0=ps[:, n, :], scalar=0.5,
                                               in1=x_sb[:, t, o:o + BANK], op0=ALU.mult, op1=ALU.add).then_inc(x2_ok, 1)
            for t in range(T):
                dve.wait_ge(tposed, KD + 2 * t + 1)
                nc.vector.tensor_copy(x2T[:, t, 0:4, :].rearrange("p k n -> p (k n)"),
                                      ps[:, 4 + 2 * t, :]).then_inc(xT_v, 1)
            inverse_variance(1, sq_sum, D, 2 * T)
            link(nc.vector.memset(rank_col[:, :, :], -1.0))

            dve.wait_ge(bias_in, 32)
            dve.wait_ge(rstd_ok, 2)
            dve.wait_ge(logit_ps, 1)
            for t in range(T):
                link(nc.vector.scalar_tensor_tensor(out=logit[:, t, :], in0=ps[:, 4, t * NE:(t + 1) * NE],
                                                    scalar=rstd[:, t:t + 1], in1=brt[:, :], op0=ALU.mult, op1=ALU.add))
            for t in range(T):
                link(nc.vector.max(top8[:, t, :], logit[:, t, :]))
                link(nc.vector.max_index(idx_u[:, t, :], top8[:, t, :], logit[:, t, :]))
            nc.vector.tensor_scalar(nmax.unsqueeze(2), top8[:, :, 0:1], -1.0, None, ALU.mult).then_inc(top_ok, 1)
            link(nc.vector.tensor_copy(idx_f, idx_u[:, :, :]))
            four = [P, T, TOPK, NE]
            link(nc.vector.tensor_tensor(hot, slotno[:, 0:NE].unsqueeze(1).unsqueeze(1).to_broadcast(four),
                                         idx_f[:, :, 0:TOPK].unsqueeze(3).to_broadcast(four), ALU.is_equal))
            nc.vector.tensor_reduce(mask, hot.rearrange("p t k e -> p t e k"), AX.X, ALU.add).then_inc(mask_ok, 1)
            dve.wait_ge(ex_ok, T)
            link(nc.vector.reciprocal(einv, esum))
            link(nc.vector.tensor_tensor(g4, ex4, einv.unsqueeze(2).to_broadcast([P, T, TOPK]), ALU.mult))
            link(nc.vector.tensor_tensor(hotg, hot, g4.unsqueeze(3).to_broadcast(four), ALU.mult))
            nc.vector.tensor_reduce(gate, hotg.rearrange("p t k e -> p t e k"), AX.X, ALU.add).then_inc(mask_ok, 1)
            dve.wait_ge(rank_ps, 1)
            link(nc.vector.scalar_tensor_tensor(out=ranked.rearrange("p t e -> p (t e)"), in0=ps[:, 5, 0:T * NE],
                                                scalar=FAR, in1=mask.rearrange("p t e -> p (t e)"),
                                                op0=ALU.add, op1=ALU.mult))

            def rank_columns(r):
                nc.vector.tensor_scalar(rank_col[:, :, r * NE:(r + 1) * NE], ranked, -FAR - CAP * r, None,
                                        ALU.add).then_inc(cols_ok, 1)

            rank_columns(0)
            dve.wait_ge(cols_ok, 1)
            for t in range(T):
                nc.vector.tensor_scalar(sel_next[:, t, :], slotno[:, 0:CAP], rank_col[:, t, 0:1], None,
                                        ALU.is_equal).then_inc(sel_ok, 1)
            link(nc.vector.tensor_reduce(cmax, ps[0:1, 5, 2 * NE:3 * NE], AX.X, ALU.max))
            link(nc.vector.tensor_scalar(rnd, cmax, float(CAP), 1.0, ALU.is_gt, ALU.add))
            for r in range(2, ROUNDS):
                link(nc.vector.tensor_scalar(rnd2, cmax, float(CAP * r), None, ALU.is_gt))
                link(nc.vector.tensor_tensor(rnd, rnd, rnd2, ALU.add))
            nc.vector.tensor_scalar(passes[:, :], rnd, float(NE), None, ALU.mult).then_inc(passes_ok, 1)
            for r in range(1, ROUNDS):
                rank_columns(r)
            dve.wait_ge(mask_ok, 2)
            for r in range(ROUNDS):
                nc.vector.tensor_copy(gate_col[:, :, r * NE:(r + 1) * NE], gate).then_inc(cols_ok, 1)
            dve.wait_ge(gateT_ps, 1)
            dve.wait_ge(zeros, 2)
            nc.vector.tensor_copy(gateT, ps[0:NE, 6, 0:TOK].rearrange("p (t n) -> p t n", t=T)).then_inc(sg_ok, 2)

            dve.wait_ge(cols_ok, 2 * ROUNDS)
            gain2 = cst[:, C_G2:C_G2 + KD].unsqueeze(2).to_broadcast([P, KD, CAP])
            dve.wait_ge(xg_ps, 1)
            nc.vector.tensor_tensor(xgT, ps[:, 7, :].rearrange("p (k n) -> p k n", k=KD), gain2,
                                    ALU.mult).then_inc(xg_ok, 1)
            gv = gub.rearrange("p (j h n) -> p j h n", j=KD, h=2)
            as3 = lambda b: b.rearrange("p (j n) -> p j n", j=KD)
            n_pass = dve.value_load(passes[0:1, 0:1], min_val=NE, max_val=NE * ROUNDS)
            with dve.Fori(0, n_pass, UNROLL) as n:
                for i in range(UNROLL):
                    n0 = dve.snap(n + i)
                    n1 = dve.snap(n + i + 1)
                    n2 = dve.snap(n + i + 2)
                    e16 = dve.snap(((n + i) & (NE - 1)) * 16)
                    dve.wait_ge(chunk_used[3], n1)
                    nc.vector.tensor_copy(gu_sb[:, 0:BANK], ps[:, 4, :]).then_inc(gu_v, 1)
                    for t in range(T):
                        nc.vector.tensor_scalar(sel_next[:, t, :], slotno[:, 0:CAP], rank_col[:, t, bass.ds(n1, 1)],
                                                None, ALU.is_equal).then_inc(sel_ok, 1)
                    for t in range(T):
                        o = i % 2 * CAP
                        nc.vector.tensor_scalar(sel_gate[:, t, o:o + CAP], slotno[:, 0:CAP],
                                                rank_col[:, t, bass.ds(n0, 1)], gate_col[:, t, bass.ds(n0, 1)],
                                                ALU.is_equal, ALU.mult).then_inc(sgate_ok, 1)
                    dve.wait_ge(tp_ps, n1)
                    nc.vector.tensor_tensor(gub.rearrange("p (j n) -> p j n", j=16),
                                            ps[:, 6:8, :].rearrange("p b (j n) -> p (b j) n", n=CAP),
                                            cst[:, bass.ds(e16 + C_BGU, 16)].unsqueeze(2).to_broadcast([P, 16, CAP]),
                                            ALU.add).then_inc(tp_read, 1)
                    dve.wait_ge(tp_read, n1)
                    nc.vector.tensor_scalar(as3(g_cl), gv[:, :, 0, :], LIMIT, None, ALU.min).then_inc(g_ok, 1)
                    nc.vector.tensor_scalar(as3(u_cl), gv[:, :, 1, :], LIMIT, -LIMIT, ALU.min, ALU.max).then_inc(u_ok, 1)
                    dve.wait_ge(g_ok, n1)
                    dve.wait_ge(u_ok, n1)
                    nc.vector.scalar_tensor_tensor(out=act1, in0=u_cl, scalar=1.0, in1=g_cl, op0=ALU.add,
                                                   op1=ALU.mult).then_inc(a1_ok, 1)
                    dve.wait_ge(a1_ok, n1)
                    dve.wait_ge(sig_ok, n1)
                    nc.vector.tensor_tensor(actT, as3(act1), as3(sig), ALU.mult).then_inc(act_ok, 1)
                    dve.wait_ge(xg_ps, n2)
                    nc.vector.tensor_tensor(xgT, ps[:, 7, :].rearrange("p (k n) -> p k n", k=KD), gain2,
                                            ALU.mult).then_inc(xg_ok, 1)
                    if i % 2 == 1:
                        dve.wait_ge(sg_ps, n1)
                        nc.vector.tensor_copy(sgT[i // 2], ps[:, 4, 0:T * P].rearrange("p (t n) -> p t n", t=T)
                                              ).then_inc(sg_ok, 2)

            for n in range(2 * T):
                t, o = n // 2, (n % 2) * BANK
                dve.wait_ge(y_ok, n + 1)
                nc.vector.tensor_tensor(x_sb[:, t, o:o + BANK], ps[:, n, :], x_sb[:, t, o:o + BANK],
                                        ALU.add).then_inc(x3_ok, 1)
            inverse_variance(2, sq_sum, D, 3 * T)
            dve.wait_ge(rstd_ok, 3)
            dve.wait_ge(late_in, 32)
            for t in range(T):
                nc.vector.scalar_tensor_tensor(out=x_sb[:, t, :], in0=x_sb[:, t, :], scalar=rstd[:, t:t + 1],
                                               in1=fin_g, op0=ALU.mult, op1=ALU.mult).then_inc(fin_ok, 1)

        @block.tensor
        def _(pe):
            def chunk_in(c):
                pe.wait_ge(split_hi, c + 1)
                pe.wait_ge(split_v, c + 1)
                pe.wait_ge(split_g, c + 1)

            def product(dst, sides, start=True, stop=True):
                for q, (a, b) in enumerate(((0, 0), (1, 0), (0, 1))):
                    for k, (st, mv) in enumerate(sides):
                        ins = nc.tensor.matmul(dst, st[a], mv[b], start=start and q == 0 and k == 0,
                                               stop=stop and q == 2 and k == len(sides) - 1)
                return ins

            def chunk(c, k):
                return [b.rearrange("p (k n) -> p k n", k=k) for b in (high(c), low(c))]

            def transposes(rows, tp0):
                for k in range(KD):
                    for t in range(T):
                        o = (k % 2) * TOK + t * P
                        ins = nc.tensor.transpose(ps[:, tp0 + k // 2, o:o + P], rows[:, t, k::KD], ident)
                    ins.then_inc(tposed, 1)

            def group(i):
                c = IN_CHUNK[i // 4]
                w = chunk(c, KD)
                if i % 4 == 0:
                    chunk_in(c)
                if i >= 4:
                    pe.wait_ge(group_read, i // 2 * 2 - 2)
                cols = slice((i % 4) * P, (i % 4 + 1) * P)
                product(half(4 + (i // 2) % 2, i % 2),
                        [([b[:, k, cols] for b in w], (hT_hi[:, k, :], hT_lo[:, k, :])) for k in range(KD)]
                        ).then_inc(group_done, 1)

            def first_groups():
                w = chunk(0, KD)
                pe.wait_ge(h_hi, 2)
                pe.wait_ge(split_hi, 1)
                for q, (a, b) in enumerate(((0, 0), (1, 0), (0, 1))):
                    if q == 1:
                        pe.wait_ge(split_v, 1)
                        pe.wait_ge(split_g, 1)
                    if q == 2:
                        pe.wait_ge(h_lo_v, 1)
                        pe.wait_ge(h_lo_g, 1)
                    for i in range(4):
                        for k in range(KD):
                            ins = nc.tensor.matmul(half(4 + i, 0), w[a][:, k, i * P:(i + 1) * P],
                                                   (hT_hi, hT_lo)[b][:, k, :],
                                                   start=(q == 0 and k == 0), stop=(q == 2 and k == KD - 1))
                        if q == 2:
                            ins.then_inc(group_done, 1)

            def lru_gate_products(u, blocks):
                pe.wait_ge(lruw_in, 16 * (u + 1))
                for c in [4 * u + b for b in blocks]:
                    pe.wait_ge(conv_ok, c + 1)
                    for m in range(4):
                        n = 4 * c + m
                        if n >= 4:
                            pe.wait_ge(gate_read, n // 2 * 2 - 2)
                        nc.tensor.matmul(half(6 + (n % 4) // 2, n % 2), lru_w_sb[:, m, c % 4, :], xc[:, c, :],
                                         start=True, stop=True).then_inc(gate_ps, 1)

            pe.wait_ge(sq_in, 16)
            pe.wait_ge(normed, T)
            transposes(hn, 0)
            first_groups()
            for i in range(4, 8):
                group(i)
            for part in range(2):
                chunk_in(Q_CHUNK + part)
                w = chunk(Q_CHUNK + part, KD)
                n_col = QW if part == 0 else 2 * KVW
                for t in range(T):
                    toks = slice(t * P, (t + 1) * P)
                    product(ps[:, 2 * t + part, 0:n_col],
                            [((hT_hi[:, k, toks], hT_lo[:, k, toks]), [b[:, k, :] for b in w]) for k in range(KD)]
                            ).then_inc(qkv_done, 1)
            lru_gate_products(0, range(4))
            for i in range(8, 14):
                group(i)
            pe.wait_ge(rot_ok, T)
            kd = k_twice.rearrange("p (t g n) -> p t g n", t=T, g=NKV)
            for j in range(2):
                for jj in range(2):
                    for t in range(T):
                        a = 2 * j + jj
                        ins = nc.tensor.transpose(ps[:, j, jj * TOK + t * P:jj * TOK + (t + 1) * P],
                                                  qkv[:, t, a * P:(a + 1) * P], ident)
                ins.then_inc(qk_tp, 1)
            for g in range(NKV):
                for t in range(T):
                    ins = nc.tensor.transpose(ps[:, 2, g * TOK + t * P:g * TOK + (t + 1) * P], kd[:, t, g, :], ident)
            ins.then_inc(qk_tp, 1)
            for i in range(14, 16):
                group(i)

            def scores(h):
                rs = slice(64 * (h % 2), 64 * (h % 2) + 64)
                if h >= 2:
                    pe.wait_ge(exp_ok, T * (h - 1))
                for t in range(T):
                    ins = nc.tensor.matmul(ps[:, h % 2, t * TOK:(t + 1) * TOK], qT[rs, h // 2, t * P:(t + 1) * P],
                                           kT[rs, h // (NQ // NKV), :], start=True, stop=True)
                ins.then_inc(score_ps, 1)

            def prob_transposes(h):
                pe.wait_ge(prob_ok, T * (h + 1))
                if h >= 1:
                    pe.wait_ge(pT_ok, h)
                for kt in range(T):
                    for t in range(T):
                        ins = nc.tensor.transpose(ps[:, 2, kt * TOK + t * P:kt * TOK + (t + 1) * P],
                                                  prob[:, h % 2, t, kt * P:(kt + 1) * P], ident)
                ins.then_inc(pT_ps, 1)

            def values(h):
                g = h // (NQ // NKV)
                o = QW + KVW + g * HD
                pe.wait_ge(pT_ok, h + 1)
                if h >= 2:
                    pe.wait_ge(attn_ok, h // 2)
                for kt in range(T):
                    ins = nc.tensor.matmul(ps[64 * (h % 2):64 * (h % 2) + 64, 3, 0:TOK],
                                           qkv[:, kt, o:o + HD], probT[:, h % 2, kt, :],
                                           start=(kt == 0), stop=(kt == T - 1))
                ins.then_inc(pv_ps, 1)

            for i in range(16, 32):
                if 17 <= i < 21:
                    lru_gate_products(1, [i - 17])
                group(i)
                s = i - 18
                if s == 0:
                    pe.wait_ge(qk_cp, 3)
                if 0 <= s - 2 < NQ:
                    prob_transposes(s - 2)
                if 0 <= s < NQ:
                    scores(s)
                if 0 <= s - 3 < NQ:
                    values(s - 3)

            BLOCKS = CH // P
            w_br = [chunk(c, BLOCKS) for c in BR_CHUNK]

            def branches(g):
                first = 12 * g
                if g == 0:
                    pe.wait_ge(rec_split, 1)
                    pe.wait_ge(group_read, 32)
                for i, c in enumerate(BR_CHUNK):
                    if first <= BLOCKS * i < first + 12:
                        chunk_in(c)
                if g >= 2:
                    pe.wait_ge(merged_ok, g - 1)
                w = [[b[:, q % BLOCKS, :] for b in w_br[q // BLOCKS]] for q in range(first, first + 12)]
                product(half(4 + g % 2, 1), [(w[k], (rec_hi[:, k, :], rec_lo[:, k, :])) for k in range(KD)])
                if g == 0:
                    pe.wait_ge(attn_split, 1)
                product(half(4 + g % 2, 0), [(w[KD + k], (attn_hi[:, k, :], attn_lo[:, k, :])) for k in range(4)]
                        ).then_inc(branch_ps, 1)

            def mix(c):
                if c % 4 == 0:
                    chunk_in(MIX_CHUNK[c // 4])
                w = chunk(MIX_CHUNK[c // 4], 4)
                pe.wait_ge(merged_ok, c + 1)
                for n in range(2 * T):
                    toks, o = slice(n // 2 * P, (n // 2 + 1) * P), (n % 2) * BANK
                    ins = product(ps[:, n, :], [((merged_hi[:, c, toks], merged_lo[:, c, toks]),
                                                 [b[:, c % 4, o:o + BANK] for b in w])],
                                  start=(c == 0), stop=(c == KD - 1))
                    if c == KD - 1 and n < 2 * T - 1:
                        ins.then_inc(mix_part, 1)
                if c % 4 == 3:
                    ins.then_inc(mixed_ps, 1)

            for g in range(5):
                branches(g)
            mix(0)
            mix(1)
            branches(5)
            mix(2)
            mix(3)
            branches(6)
            branches(7)
            for c in range(4, KD):
                mix(c)

            for t in range(T):
                pe.wait_ge(x2_ok, 2 * t + 2)
                for k in range(KD):
                    o = (k % 4) * P
                    ins = nc.tensor.transpose(ps[:, 4 + 2 * t + k // 4, o:o + P], x_sb[:, t, k::KD], ident)
                    if k % 4 == 3:
                        ins.then_inc(tposed, 1)
            pe.wait_ge(wrg_ok, 1)
            for t in range(T):
                pe.wait_ge(xT_v, t + 1)
                pe.wait_ge(xT_a, t + 1)
                for k in range(KD):
                    ins = nc.tensor.matmul(ps[:, 4, t * NE:(t + 1) * NE], x2T[:, t, k, :], wrg[:, k, :],
                                           start=(k == 0), stop=(k == KD - 1))
            ins.then_inc(logit_ps, 1)
            pe.wait_ge(zeros, 2)
            nothing = sgT[0].rearrange("p t n -> p (t n)").bitcast(bf16)
            for n in range(2 * T):
                nc.tensor.matmul(ps[:, n, :], nothing[:, 0:P], nothing[:, 0:BANK], start=True, stop=False)
            pe.wait_ge(mask_ok, 1)
            pe.wait_ge(xT_a, T)
            nc.tensor.matmul(ps[:, 5, 0:NE], upper, mask[:, 0, :], start=True, stop=True)
            nc.tensor.matmul(ps[:, 5, NE:2 * NE], ones, mask[:, 0, :], start=True, stop=False)
            nc.tensor.matmul(ps[:, 5, NE:2 * NE], upper, mask[:, 1, :], start=False, stop=True)
            for t in range(T):
                ins = nc.tensor.matmul(ps[:, 5, 2 * NE:3 * NE], ones, mask[:, t, :], start=(t == 0), stop=(t == T - 1))
            ins.then_inc(rank_ps, 1)
            pe.wait_ge(mask_ok, 2)
            for t in range(T):
                ins = nc.tensor.transpose(ps[0:NE, 6, t * P:(t + 1) * P], gate[:, t, :], ident)
            ins.then_inc(gateT_ps, 1)

            def gather():
                for k in range(KD):
                    for t in range(T):
                        ins = nc.tensor.matmul(ps[:, 7, k * CAP:(k + 1) * CAP], hn[:, t, k::KD], sel_next[:, t, :],
                                               start=(t == 0), stop=(t == T - 1))
                return ins

            pe.wait_ge(sel_ok, T)
            pe.wait_ge(normed, 2 * T)
            gather().then_inc(xg_ps, 1)
            pe.wait_ge(sg_ok, 2)
            pe.wait_ge(late_in, 32)

            def scatter(pair, n, last=False):
                return nc.tensor.matmul(ps[:, n, :], sgT[pair][:, n // 2, :],
                                        pair_out[pair][:, (n % 2) * BANK:(n % 2 + 1) * BANK], start=False, stop=last)

            n_pass = pe.value_load(passes[0:1, 0:1], min_val=NE, max_val=NE * ROUNDS)
            with pe.Fori(0, n_pass, UNROLL) as n:
                for i in range(UNROLL):
                    n1 = pe.snap(n + i + 1)
                    n2 = pe.snap(n + i + 2)
                    sel_n = pe.snap((n + i) * T + 2 * T)
                    use = [EARLIER[SLOT_ORDER[(PER * i + j) % SLOTS]] + (PER * i + j) // SLOTS + 1 for j in range(PER)]
                    full = {u: pe.snap(n * (16 * PER // SLOTS) + 16 * u) for u in sorted(set(use))}
                    if i % 2 == 0:
                        out_n = pe.snap((n + i) * 2 + 1)
                    else:
                        sgate_n = pe.snap((n + i) * T + T)
                    last_pair = (i // 2 + 1) % 2
                    pe.wait_ge(xg_ok, n1)
                    if i % 2 == 0:
                        pe.wait_ge(sg_ok, n2)
                    for j in range(4):
                        s = SLOT_ORDER[(PER * i + j) % SLOTS]
                        pe.wait_ge(slot_full[s], full[use[j]])
                        w = slot(s).rearrange("p (r n) -> p r n", r=2)
                        for r in range(2):
                            k = 2 * j + r
                            for b in range(2):
                                for side in range(2):
                                    o = side * FF + b * BANK
                                    ins = nc.tensor.matmul(ps[64 * side:64 * side + 64, 4 + b, :], xgT[:, k, :],
                                                           w[:, r, o:o + BANK], start=(k == 0), stop=(k == KD - 1))
                        ins.then_inc(chunk_used[j], 1)
                    if i % 2 == 0:
                        pe.wait_ge(out_ok, out_n)
                    scatter(last_pair, 2 * (i % 2))
                    pe.wait_ge(gu_v, n1)
                    pe.wait_ge(gu_a, n1)
                    for j in range(KD):
                        o = (j % 4) * P
                        ins = nc.tensor.transpose(ps[:, 6 + j // 4, o:o + P], gu_sb[:, j::KD], ident)
                    ins.then_inc(tp_ps, 1)
                    scatter(last_pair, 2 * (i % 2) + 1)
                    pe.wait_ge(sel_ok, sel_n)
                    pe.wait_ge(tp_read, n1)
                    gather().then_inc(xg_ps, 1)
                    if i % 2 == 1:
                        pe.wait_ge(sgate_ok, sgate_n)
                        for t in range(T):
                            ins = nc.tensor.transpose(ps[:, 4, t * P:(t + 1) * P], sel_gate[:, t, :], ident)
                        ins.then_inc(sg_ps, 2)
                    pe.wait_ge(act_ok, n1)
                    for j in range(4, PER):
                        s = SLOT_ORDER[(PER * i + j) % SLOTS]
                        pe.wait_ge(slot_full[s], full[use[j]])
                        w = slot(s).rearrange("p (r n) -> p r n", r=4)
                        for r in range(4):
                            k = 4 * (j - 4) + r
                            for side in range(2):
                                ins = nc.tensor.matmul(ps[64 * side:64 * side + 64, 6, :], actT[:, k, :],
                                                       w[:, r, side * BANK:(side + 1) * BANK],
                                                       start=(k == 0), stop=(k == KD - 1))
                        ins.then_inc(chunk_used[j], 1)
            last = pe.snap(n_pass * 2 + 1)
            last_sg = pe.snap(n_pass + 2)
            pe.wait_ge(out_ok, last)
            pe.wait_ge(sg_ok, last_sg)
            for n in range(2 * T):
                scatter(1, n, True).then_inc(y_ok, 1)


def _layouts(a):
    w_in = a["w_in"][0].reshape(P, KD, -1)
    o = QKV
    parts = [w_in[:, :, o:o + 512], w_in[:, :, o + 512:o + 1024], w_in[:, :, 0:QW]]
    gates = np.zeros((2, P, 4, 4, P), np.float32)
    for m, w in enumerate((a["lru_wa"][0, 0], a["lru_wi"][0, 0], a["lru_wa"][0, 1], a["lru_wi"][0, 1])):
        for r in range(2):
            rs = slice(64 * r, 64 * r + 64)
            gates[:, rs, m, :, rs] = w[r::2].reshape(2, 4, 64, 64).transpose(0, 2, 1, 3)
    kv = w_in[:, :, QW:QKV].reshape(P, -1)
    kv = np.concatenate([kv, np.zeros((P, CH - kv.shape[1]), np.float32)], axis=1)
    rest = [w_in[:, :, o + 1024 + 512 * i:o + 1536 + 512 * i] for i in range(6)]
    mix = [w.transpose(1, 0, 2) for w in a["w_out"][0].reshape(2, 4, P, D)]
    both = np.concatenate([a["w_lru_o"][0], a["w_attn_o"][0]]).reshape(12, P, KD, P).transpose(1, 2, 0, 3)
    both = both.reshape(P, 3, CH).transpose(1, 0, 2)
    chunks = parts + [kv] + rest + [both[0], both[1], mix[0], both[2], mix[1]]
    pre = np.stack([np.ascontiguousarray(c).reshape(P, CH) for c in chunks])

    chan = lambda v: v.reshape(-1, P).T
    rows = TOK // GRID_W
    f32 = np.float32
    inv = THETA ** (-np.arange(0, HD // 2, 2, dtype=f32) / (HD // 2))
    row = np.repeat(np.arange(rows), GRID_W).astype(f32)
    colm = np.tile(np.arange(GRID_W), rows).astype(f32)
    ang_r, ang_c = row[:, None] * inv[None], colm[:, None] * inv[None]
    cos = np.concatenate([np.cos(ang_r)] * 2 + [np.cos(ang_c)] * 2, axis=1).astype(f32)
    sin = np.concatenate([-np.sin(ang_r), np.sin(ang_r), -np.sin(ang_c), np.sin(ang_c)], axis=1).astype(f32)
    tiles = lambda t: t.reshape(T, P, HD).transpose(1, 0, 2).reshape(P, -1)
    lb = np.concatenate([chan(a[k][0, d]) for d in range(2) for k in ("lru_ba", "lru_bi")], axis=1)
    bgu = a["b_gu"][0].reshape(NE, 2, P, KD).transpose(2, 0, 3, 1).reshape(P, -1)
    wr = a["w_router"][0].reshape(P, KD * NE)
    consts = np.concatenate([
        a["norm1_g"][0].reshape(P, KD), a["norm2_g"][0].reshape(P, KD), chan(a["b_in"][0][QKV:]),
        *[chan(a["conv_w"][0, j]) for j in range(TAPS)], chan(a["conv_b"][0]), lb,
        chan(a["lru_lambda"][0, 0]), chan(a["lru_lambda"][0, 1]), tiles(cos), tiles(sin), bgu, wr], axis=1)
    squares = np.stack([np.eye(P), np.triu(np.ones((P, P)), 1), np.ones((P, P)),
                        np.tile(np.arange(CAP), (P, P // CAP))], axis=1).astype(f32)
    one_row = np.concatenate([a["b_in"][0][:QKV], np.tile(a["q_norm_g"][0], NQ), np.tile(a["k_norm_g"][0], NKV), a["b_router"][0],
                              a["final_g"]])[None]
    return {"x": a["x"].reshape(TOK, D), "consts": consts, "squares": squares, "rows": one_row, "pre": pre,
            "w_lru": gates.reshape(2, P, -1),
            "w_gu": a["w_gu"][0], "w_down": a["w_down"][0], "b_down": a["b_down"][0]}


def kernel(**inputs):
    import concourse.bacc as _bacc
    from concourse.bass_utils import run_bass_kernel_spmd as _run

    arrays = _layouts({k: np.asarray(v) for k, v in inputs.items()})
    nc = _bacc.Bacc("TRN2", target_bir_lowering=False, num_devices=1, dynamic_dma_scratch_size=1024)
    feed, args = {}, []
    for name, a in arrays.items():
        a = np.ascontiguousarray(a)
        feed[f"in_{name}_dram"] = a
        args.append(nc.dram_tensor(f"in_{name}_dram", a.shape, mybir.dt.from_np(a.dtype), kind="ExternalInput").ap())
    args.append(nc.dram_tensor("out_0_dram", (TOK, D), mybir.dt.float32, kind="ExternalOutput").ap())
    encoder_layer(nc, *args)
    r = _run(nc, [feed], core_ids=[0])
    return r.results[0]["out_0_dram"].reshape(1, TOK, D)
```
